# Optimizing a Trainium2 kernel written in Bass

```python
import jax, jax.numpy as jnp
from jax import lax
import numpy as np
import math

D_MODEL = 1024
BATCH = 1
SEQ = 256
DEPTH = 2

CHUNK = 64
LEFT_CHUNKS = 8
BAND = (LEFT_CHUNKS + 1) * CHUNK
HEAD_DIM = 64
N_HEADS_A = 8
N_HEADS_C = 8
WIDTH_A = N_HEADS_A * HEAD_DIM
WIDTH_C = N_HEADS_C * HEAD_DIM
POOL_WINDOWS = (2, 4, 8, 16)
N_POOL_GROUPS = 4
POOL_GROUP_DIM = 128
WIDTH_B = N_POOL_GROUPS * POOL_GROUP_DIM
REL_CLIP = 128
N_REL = 2 * REL_CLIP + 1
N_BRANCHES = 3
D_FF = 2816
Q_BLOCK = 128
N_MOD = 9
EPS = 1e-6
NEG_INF = -1e30

SPLIT_SIZES = (WIDTH_A, WIDTH_A, WIDTH_A, WIDTH_B, WIDTH_C, WIDTH_C, WIDTH_C, N_HEADS_C, N_BRANCHES * D_MODEL)
D_IN = sum(SPLIT_SIZES)
SPLIT_POINTS = tuple(int(p) for p in np.cumsum(SPLIT_SIZES)[:-1])


def rms_norm(x, gain):
    xf = x.astype(jnp.float32)
    y = xf * lax.rsqrt(jnp.mean(xf * xf, axis=-1, keepdims=True) + EPS)
    return (y * gain.astype(jnp.float32)).astype(x.dtype)

def modulate(h, shift, scale):
    return h * (1 + scale[:, None, :]) + shift[:, None, :]

def swiglu(h, w_gate, w_up, w_down):
    return (jax.nn.silu(h @ w_gate) * (h @ w_up)) @ w_down

def chunked_relpos_attention(q, k, v, gq, gk, rel_bias):
    B, S, H, dh = q.shape
    nc = S // CHUNK
    qf = rms_norm(q, gq).astype(jnp.float32) * (dh ** -0.5)
    kf = rms_norm(k, gk).astype(jnp.float32)
    qc = qf.reshape(B, nc, CHUNK, H, dh)
    pad = ((0, 0), (LEFT_CHUNKS * CHUNK, 0), (0, 0), (0, 0))
    kp = jnp.pad(kf, pad).reshape(B, nc + LEFT_CHUNKS, CHUNK, H, dh)
    vp = jnp.pad(v, pad).reshape(B, nc + LEFT_CHUNKS, CHUNK, H, dh)
    band_idx = np.arange(nc)[:, None] + np.arange(LEFT_CHUNKS + 1)[None, :]
    kb = kp[:, band_idx].reshape(B, nc, BAND, H, dh)
    vb = vp[:, band_idx].reshape(B, nc, BAND, H, dh)
    logits = jnp.einsum('bnqhd,bnkhd->bhnqk', qc, kb)
    rel = np.arange(CHUNK)[:, None] + LEFT_CHUNKS * CHUNK - np.arange(BAND)[None, :]
    rel_idx = np.clip(rel, -REL_CLIP, REL_CLIP) + REL_CLIP
    bias = rel_bias[:, rel_idx].astype(jnp.float32)
    valid = np.repeat(band_idx >= LEFT_CHUNKS, CHUNK, axis=1)
    logits = jnp.where(valid[None, None, :, None, :], logits + bias[None, :, None], NEG_INF)
    p = jax.nn.softmax(logits, axis=-1).astype(v.dtype)
    out = jnp.einsum('bhnqk,bnkhd->bnqhd', p, vb)
    return out.reshape(B, S, H * dh)

def multiscale_pool(u, w_pool, pool_scale):
    B, S, _ = u.shape
    uf = u.astype(jnp.float32)
    cs = jnp.concatenate([jnp.zeros((B, 1, WIDTH_B), jnp.float32), jnp.cumsum(uf, axis=1)], axis=1)
    t = jnp.arange(S, dtype=jnp.float32)
    diffs = []
    for g, w in enumerate(POOL_WINDOWS):
        sl = slice(g * POOL_GROUP_DIM, (g + 1) * POOL_GROUP_DIM)
        csg = cs[:, :, sl]
        upper = csg[:, 1:]
        lower = jnp.pad(csg[:, :S + 1 - w], ((0, 0), (w - 1, 0), (0, 0)))
        count = jnp.minimum(t + 1, float(w))[None, :, None]
        diffs.append((upper - lower) / count - uf[:, :, sl])
    d = jnp.stack(diffs, axis=2).astype(u.dtype)
    y = jnp.einsum('bsgc,gce->bsge', d, w_pool).reshape(B, S, WIDTH_B)
    return y * pool_scale

def forgetting_attention(q, k, v, gq, gk, f_logit):
    B, S, H, dh = q.shape
    qf = rms_norm(q, gq).astype(jnp.float32) * (dh ** -0.5)
    kf = rms_norm(k, gk).astype(jnp.float32)
    cum_logf = jnp.cumsum(jax.nn.log_sigmoid(f_logit.astype(jnp.float32)), axis=1)
    cum_k = cum_logf.transpose(0, 2, 1)
    kpos = jnp.arange(S)

    def block(i):
        start = i * Q_BLOCK
        qb = lax.dynamic_slice_in_dim(qf, start, Q_BLOCK, axis=1)
        cq = lax.dynamic_slice_in_dim(cum_k, start, Q_BLOCK, axis=2)
        logits = jnp.einsum('bqhd,bkhd->bhqk', qb, kf) + (cq[..., None] - cum_k[:, :, None, :])
        qpos = start + jnp.arange(Q_BLOCK)
        mask = kpos[None, :] <= qpos[:, None]
        logits = jnp.where(mask[None, None], logits, NEG_INF)
        p = jax.nn.softmax(logits, axis=-1).astype(v.dtype)
        return jnp.einsum('bhqk,bkhd->bqhd', p, v)

    out = lax.map(block, jnp.arange(S // Q_BLOCK))
    return out.transpose(1, 0, 2, 3, 4).reshape(B, S, H * dh)

def hybrid_mixer(h, w_in, qk_gain, rel_bias, forget_bias, w_pool, pool_scale, w_branch, w_out):
    B, S, _ = h.shape
    proj = h @ w_in
    qa, ka, va, ub, qc, kc, vc, f_lin, g_lin = jnp.split(proj, SPLIT_POINTS, axis=-1)
    ha = lambda t: t.reshape(B, S, N_HEADS_A, HEAD_DIM)
    hc = lambda t: t.reshape(B, S, N_HEADS_C, HEAD_DIM)
    ya = chunked_relpos_attention(ha(qa), ha(ka), ha(va), qk_gain[0], qk_gain[1], rel_bias)
    yb = multiscale_pool(ub, w_pool, pool_scale)
    yc = forgetting_attention(hc(qc), hc(kc), hc(vc), qk_gain[2], qk_gain[3], f_lin + forget_bias)
    ys = jnp.stack([ya, yb, yc], axis=2)
    branch = jnp.einsum('bsnw,nwd->bsnd', ys, w_branch)
    gates = jax.nn.sigmoid(g_lin.reshape(B, S, N_BRANCHES, D_MODEL))
    merged = jnp.sum(gates * branch, axis=2)
    return merged @ w_out

def first_inputs(seed: int = 0) -> dict:
    key = jax.random.key(seed)
    ks = jax.random.split(key, 18)
    nrm = lambda k, shape, s: jax.random.normal(k, shape, jnp.float32) * s
    return {
        "x": nrm(ks[0], (BATCH, SEQ, D_MODEL), 1.0),
        "c": nrm(ks[1], (BATCH, D_MODEL), 1.0),
        "w_ada": nrm(ks[2], (DEPTH, D_MODEL, N_MOD * D_MODEL), 0.5 * D_MODEL ** -0.5),
        "b_ada": nrm(ks[3], (DEPTH, N_MOD * D_MODEL), 0.02),
        "norm_gain": 1.0 + nrm(ks[4], (DEPTH, 3, D_MODEL), 0.05),
        "ffn_w_gate": nrm(ks[5], (DEPTH, 2, D_MODEL, D_FF), D_MODEL ** -0.5),
        "ffn_w_up": nrm(ks[6], (DEPTH, 2, D_MODEL, D_FF), D_MODEL ** -0.5),
        "ffn_w_down": nrm(ks[7], (DEPTH, 2, D_FF, D_MODEL), D_FF ** -0.5),
        "w_in": nrm(ks[8], (DEPTH, D_MODEL, D_IN), D_MODEL ** -0.5),
        "qk_gain": 1.0 + nrm(ks[9], (DEPTH, 4, HEAD_DIM), 0.05),
        "rel_bias": nrm(ks[10], (DEPTH, N_HEADS_A, N_REL), 0.5),
        "forget_bias": 1.0 + 3.0 * jax.random.uniform(ks[11], (DEPTH, N_HEADS_C), jnp.float32),
        "w_pool": nrm(ks[12], (DEPTH, N_POOL_GROUPS, POOL_GROUP_DIM, POOL_GROUP_DIM), POOL_GROUP_DIM ** -0.5),
        "pool_scale": 1.0 + nrm(ks[13], (DEPTH, WIDTH_B), 0.05),
        "w_branch": nrm(ks[14], (DEPTH, N_BRANCHES, WIDTH_A, D_MODEL), WIDTH_A ** -0.5),
        "w_out": nrm(ks[15], (DEPTH, D_MODEL, D_MODEL), D_MODEL ** -0.5),
    }

def first_block(x, c, w_ada, b_ada, norm_gain, ffn_w_gate, ffn_w_up, ffn_w_down, w_in, qk_gain,
              rel_bias, forget_bias, w_pool, pool_scale, w_branch, w_out):
    B = x.shape[0]
    c_act = jax.nn.silu(c)
    for l in range(DEPTH):
        mod = (c_act @ w_ada[l] + b_ada[l]).reshape(B, N_MOD, D_MODEL)
        h = modulate(rms_norm(x, norm_gain[l, 0]), mod[:, 0], mod[:, 1])
        x = x + 0.5 * mod[:, 2][:, None, :] * swiglu(h, ffn_w_gate[l, 0], ffn_w_up[l, 0], ffn_w_down[l, 0])
        h = modulate(rms_norm(x, norm_gain[l, 1]), mod[:, 3], mod[:, 4])
        x = x + mod[:, 5][:, None, :] * hybrid_mixer(h, w_in[l], qk_gain[l], rel_bias[l], forget_bias[l],
                                                      w_pool[l], pool_scale[l], w_branch[l], w_out[l])
        h = modulate(rms_norm(x, norm_gain[l, 2]), mod[:, 6], mod[:, 7])
        x = x + 0.5 * mod[:, 8][:, None, :] * swiglu(h, ffn_w_gate[l, 1], ffn_w_up[l, 1], ffn_w_down[l, 1])
    return x


DEPTH_2 = 4

N_MIXERS = 3
N_CONV_LAYERS = (DEPTH_2 + 2) // 3
N_LRU_LAYERS = (DEPTH_2 + 1) // 3
N_MLA_LAYERS = DEPTH_2 // 3

CONV_WIDTH = 3

LRU_WIDTH = 1280
LRU_BLOCKS = 10
LRU_BLOCK_W = LRU_WIDTH // LRU_BLOCKS
LRU_CONV_WIDTH = 4
LRU_C = 8.0

MLA_HEADS = 8
Q_LORA_RANK = 384
KV_LORA_RANK = 256
QK_NOPE_DIM = 128
QK_ROPE_DIM = 64
V_HEAD_DIM = 128
ROPE_THETA = 10000.0

D_FF_2 = ((8 * D_MODEL // 3 + 255) // 256) * 256

NORM_EPS = 1e-6


def rms_norm_2(x, g):
    xf = x.astype(jnp.float32)
    y = xf * lax.rsqrt(jnp.mean(xf * xf, axis=-1, keepdims=True) + NORM_EPS)
    return (y * g.astype(jnp.float32)).astype(x.dtype)

def causal_depthwise_conv(x, w):
    width, ch = w.shape
    return lax.conv_general_dilated(
        x, w[:, None, :].astype(x.dtype), window_strides=(1,),
        padding=[(width - 1, 0)], dimension_numbers=('NWC', 'WIO', 'NWC'),
        feature_group_count=ch)

def short_conv_mixer(xn, w_in, w_conv, w_out):
    b_gate, c_gate, h = jnp.split(xn @ w_in, 3, axis=-1)
    y = b_gate * causal_depthwise_conv(c_gate * h, w_conv)
    return y @ w_out

def rg_lru(xs, wa, ba, wx, bx, lam):
    bsz, seq, width = xs.shape
    xb = xs.reshape(bsz, seq, LRU_BLOCKS, LRU_BLOCK_W)
    r = jax.nn.sigmoid(jnp.einsum('bsnd,nde->bsne', xb, wa) + ba).reshape(bsz, seq, width)
    i = jax.nn.sigmoid(jnp.einsum('bsnd,nde->bsne', xb, wx) + bx).reshape(bsz, seq, width)
    log_a = LRU_C * r.astype(jnp.float32) * jax.nn.log_sigmoid(lam.astype(jnp.float32))
    a = jnp.exp(log_a)
    mult = jnp.sqrt(-jnp.expm1(2.0 * log_a))
    b = mult * (i * xs).astype(jnp.float32)

    def combine(left, right):
        a_l, b_l = left
        a_r, b_r = right
        return a_l * a_r, a_r * b_l + b_r

    _, h = lax.associative_scan(combine, (a, b), axis=1)
    return h.astype(xs.dtype)

def recurrent_mixer(xn, w_in, conv_w, conv_b, gate_a_w, gate_a_b, gate_x_w, gate_x_b, lam, w_out):
    gate_branch, rec_branch = jnp.split(xn @ w_in, 2, axis=-1)
    gate = jax.nn.gelu(gate_branch, approximate=True)
    rec = causal_depthwise_conv(rec_branch, conv_w) + conv_b
    h = rg_lru(rec, gate_a_w, gate_a_b, gate_x_w, gate_x_b, lam)
    return (gate * h) @ w_out

def apply_rope(t, cos, sin):
    half = t.shape[-1] // 2
    tf = t.astype(jnp.float32)
    t1, t2 = tf[..., :half], tf[..., half:]
    return jnp.concatenate([t1 * cos - t2 * sin, t2 * cos + t1 * sin], axis=-1).astype(t.dtype)

def mla_mixer(xn, cos, sin, w_down, q_norm, kv_norm, w_uq, w_ukv,
              qn_norm, qr_norm, kn_norm, kr_norm, w_o):
    bsz, seq, _ = xn.shape
    c = xn @ w_down
    c_q = c[..., :Q_LORA_RANK]
    c_kv = c[..., Q_LORA_RANK:Q_LORA_RANK + KV_LORA_RANK]
    k_rope = c[..., Q_LORA_RANK + KV_LORA_RANK:]

    q = (rms_norm_2(c_q, q_norm) @ w_uq).reshape(bsz, seq, MLA_HEADS, QK_NOPE_DIM + QK_ROPE_DIM)
    kv = (rms_norm_2(c_kv, kv_norm) @ w_ukv).reshape(bsz, seq, MLA_HEADS, QK_NOPE_DIM + V_HEAD_DIM)
    q_nope = rms_norm_2(q[..., :QK_NOPE_DIM], qn_norm)
    q_rope = apply_rope(rms_norm_2(q[..., QK_NOPE_DIM:], qr_norm), cos[:, :, None, :], sin[:, :, None, :])
    k_nope = rms_norm_2(kv[..., :QK_NOPE_DIM], kn_norm)
    v = kv[..., QK_NOPE_DIM:]
    k_rope = apply_rope(rms_norm_2(k_rope, kr_norm), cos, sin)

    scale = 1.0 / math.sqrt(QK_NOPE_DIM + QK_ROPE_DIM)
    n_blk = seq // Q_BLOCK

    def to_blocks(t):
        return t.reshape(bsz, n_blk, Q_BLOCK, *t.shape[2:]).transpose(1, 0, 2, 3, 4)

    k_idx = jnp.arange(seq)

    def attend(args):
        qn_b, qr_b, start = args
        s = (jnp.einsum('bqhd,bkhd->bhqk', qn_b, k_nope)
             + jnp.einsum('bqhr,bkr->bhqk', qr_b, k_rope)).astype(jnp.float32) * scale
        q_idx = start + jnp.arange(Q_BLOCK)
        mask = k_idx[None, :] <= q_idx[:, None]
        s = jnp.where(mask, s, jnp.finfo(jnp.float32).min)
        p = jax.nn.softmax(s, axis=-1).astype(v.dtype)
        return jnp.einsum('bhqk,bkhd->bqhd', p, v)

    starts = jnp.arange(n_blk, dtype=jnp.int32) * Q_BLOCK
    o = lax.map(attend, (to_blocks(q_nope), to_blocks(q_rope), starts))
    o = o.transpose(1, 0, 2, 3, 4).reshape(bsz, seq, MLA_HEADS * V_HEAD_DIM)
    return o @ w_o

def swiglu_ffn(xn, w_gu, w_down):
    gate, up = jnp.split(xn @ w_gu, 2, axis=-1)
    return (jax.nn.silu(gate) * up) @ w_down

def second_inputs(seed: int = 0) -> dict:
    key = jax.random.key(seed)
    ks = iter(jax.random.split(key, 40))
    f32 = jnp.float32
    res = (2 * DEPTH_2) ** -0.5

    def nrm(shape, scale):
        return jax.random.normal(next(ks), shape, f32) * scale

    def gain(shape):
        return 1.0 + 0.05 * jax.random.normal(next(ks), shape, f32)

    x = jax.random.normal(next(ks), (BATCH, SEQ, D_MODEL), f32)
    offset = jax.random.randint(next(ks), (BATCH, 1), 0, 1024, dtype=jnp.int32)
    positions = offset + jnp.arange(SEQ, dtype=jnp.int32)[None, :]

    mix_norm = gain((DEPTH_2, D_MODEL))

    nA = N_CONV_LAYERS
    conv_w_in = nrm((nA, D_MODEL, 3 * D_MODEL), D_MODEL ** -0.5)
    conv_w = nrm((nA, CONV_WIDTH, D_MODEL), CONV_WIDTH ** -0.5)
    conv_w_out = nrm((nA, D_MODEL, D_MODEL), D_MODEL ** -0.5 * res)

    nB = N_LRU_LAYERS
    lru_w_in = nrm((nB, D_MODEL, 2 * LRU_WIDTH), D_MODEL ** -0.5)
    lru_conv_w = nrm((nB, LRU_CONV_WIDTH, LRU_WIDTH), LRU_CONV_WIDTH ** -0.5)
    lru_conv_b = nrm((nB, LRU_WIDTH), 0.01)
    lru_gate_a_w = nrm((nB, LRU_BLOCKS, LRU_BLOCK_W, LRU_BLOCK_W), LRU_BLOCK_W ** -0.5)
    lru_gate_a_b = nrm((nB, LRU_BLOCKS, LRU_BLOCK_W), 0.01)
    lru_gate_x_w = nrm((nB, LRU_BLOCKS, LRU_BLOCK_W, LRU_BLOCK_W), LRU_BLOCK_W ** -0.5)
    lru_gate_x_b = nrm((nB, LRU_BLOCKS, LRU_BLOCK_W), 0.01)
    a0 = jax.random.uniform(next(ks), (nB, LRU_WIDTH), f32, 0.9, 0.999)
    lru_lambda = jnp.log(a0) - jnp.log1p(-a0)
    lru_w_out = nrm((nB, LRU_WIDTH, D_MODEL), LRU_WIDTH ** -0.5 * res)

    nC = N_MLA_LAYERS
    mla_w_down = nrm((nC, D_MODEL, Q_LORA_RANK + KV_LORA_RANK + QK_ROPE_DIM), D_MODEL ** -0.5)
    mla_q_norm = gain((nC, Q_LORA_RANK))
    mla_kv_norm = gain((nC, KV_LORA_RANK))
    mla_w_uq = nrm((nC, Q_LORA_RANK, MLA_HEADS * (QK_NOPE_DIM + QK_ROPE_DIM)), Q_LORA_RANK ** -0.5)
    mla_w_ukv = nrm((nC, KV_LORA_RANK, MLA_HEADS * (QK_NOPE_DIM + V_HEAD_DIM)), KV_LORA_RANK ** -0.5)
    mla_qn_norm = gain((nC, QK_NOPE_DIM))
    mla_qr_norm = gain((nC, QK_ROPE_DIM))
    mla_kn_norm = gain((nC, QK_NOPE_DIM))
    mla_kr_norm = gain((nC, QK_ROPE_DIM))
    mla_w_o = nrm((nC, MLA_HEADS * V_HEAD_DIM, D_MODEL), (MLA_HEADS * V_HEAD_DIM) ** -0.5 * res)

    ffn_norm = gain((DEPTH_2, D_MODEL))
    ffn_w_gu = nrm((DEPTH_2, D_MODEL, 2 * D_FF_2), D_MODEL ** -0.5)
    ffn_w_down = nrm((DEPTH_2, D_FF_2, D_MODEL), D_FF_2 ** -0.5 * res)

    return {'x': x, 'positions': positions, 'mix_norm': mix_norm,
            'conv_w_in': conv_w_in, 'conv_w': conv_w, 'conv_w_out': conv_w_out,
            'lru_w_in': lru_w_in, 'lru_conv_w': lru_conv_w, 'lru_conv_b': lru_conv_b,
            'lru_gate_a_w': lru_gate_a_w, 'lru_gate_a_b': lru_gate_a_b,
            'lru_gate_x_w': lru_gate_x_w, 'lru_gate_x_b': lru_gate_x_b,
            'lru_lambda': lru_lambda, 'lru_w_out': lru_w_out,
            'mla_w_down': mla_w_down, 'mla_q_norm': mla_q_norm, 'mla_kv_norm': mla_kv_norm,
            'mla_w_uq': mla_w_uq, 'mla_w_ukv': mla_w_ukv,
            'mla_qn_norm': mla_qn_norm, 'mla_qr_norm': mla_qr_norm,
            'mla_kn_norm': mla_kn_norm, 'mla_kr_norm': mla_kr_norm, 'mla_w_o': mla_w_o,
            'ffn_norm': ffn_norm, 'ffn_w_gu': ffn_w_gu, 'ffn_w_down': ffn_w_down}

def second_block(x, positions, mix_norm, conv_w_in, conv_w, conv_w_out,
              lru_w_in, lru_conv_w, lru_conv_b, lru_gate_a_w, lru_gate_a_b,
              lru_gate_x_w, lru_gate_x_b, lru_lambda, lru_w_out,
              mla_w_down, mla_q_norm, mla_kv_norm, mla_w_uq, mla_w_ukv,
              mla_qn_norm, mla_qr_norm, mla_kn_norm, mla_kr_norm, mla_w_o,
              ffn_norm, ffn_w_gu, ffn_w_down):
    inv_freq = ROPE_THETA ** (-jnp.arange(0, QK_ROPE_DIM, 2, dtype=jnp.float32) / QK_ROPE_DIM)
    angle = positions.astype(jnp.float32)[..., None] * inv_freq
    cos, sin = jnp.cos(angle), jnp.sin(angle)

    h = x
    for i in range(DEPTH_2):
        kind, j = i % N_MIXERS, i // N_MIXERS
        xn = rms_norm_2(h, mix_norm[i])
        if kind == 0:
            y = short_conv_mixer(xn, conv_w_in[j], conv_w[j], conv_w_out[j])
        elif kind == 1:
            y = recurrent_mixer(xn, lru_w_in[j], lru_conv_w[j], lru_conv_b[j],
                                lru_gate_a_w[j], lru_gate_a_b[j], lru_gate_x_w[j],
                                lru_gate_x_b[j], lru_lambda[j], lru_w_out[j])
        else:
            y = mla_mixer(xn, cos, sin, mla_w_down[j], mla_q_norm[j], mla_kv_norm[j],
                          mla_w_uq[j], mla_w_ukv[j], mla_qn_norm[j], mla_qr_norm[j],
                          mla_kn_norm[j], mla_kr_norm[j], mla_w_o[j])
        h = h + y
        h = h + swiglu_ffn(rms_norm_2(h, ffn_norm[i]), ffn_w_gu[i], ffn_w_down[i])
    return h


def setup_inputs(seed=0):
    out = dict(first_inputs(seed))
    for name, value in second_inputs(seed + 1).items():
        if name != "x":
            out[name + "_2"] = value
    return out


def reference(
    x, c, w_ada, b_ada, norm_gain, ffn_w_gate, ffn_w_up, ffn_w_down, w_in, qk_gain, rel_bias,
    forget_bias, w_pool, pool_scale, w_branch, w_out, positions_2, mix_norm_2, conv_w_in_2,
    conv_w_2, conv_w_out_2, lru_w_in_2, lru_conv_w_2, lru_conv_b_2, lru_gate_a_w_2,
    lru_gate_a_b_2, lru_gate_x_w_2, lru_gate_x_b_2, lru_lambda_2, lru_w_out_2, mla_w_down_2,
    mla_q_norm_2, mla_kv_norm_2, mla_w_uq_2, mla_w_ukv_2, mla_qn_norm_2, mla_qr_norm_2,
    mla_kn_norm_2, mla_kr_norm_2, mla_w_o_2, ffn_norm_2, ffn_w_gu_2, ffn_w_down_2,
):
    x = first_block(
        x, c, w_ada, b_ada, norm_gain, ffn_w_gate, ffn_w_up, ffn_w_down, w_in, qk_gain,
        rel_bias, forget_bias, w_pool, pool_scale, w_branch, w_out,
    )
    return second_block(
        x, positions_2, mix_norm_2, conv_w_in_2, conv_w_2, conv_w_out_2, lru_w_in_2,
        lru_conv_w_2, lru_conv_b_2, lru_gate_a_w_2, lru_gate_a_b_2, lru_gate_x_w_2,
        lru_gate_x_b_2, lru_lambda_2, lru_w_out_2, mla_w_down_2, mla_q_norm_2, mla_kv_norm_2,
        mla_w_uq_2, mla_w_ukv_2, mla_qn_norm_2, mla_qr_norm_2, mla_kn_norm_2, mla_kr_norm_2,
        mla_w_o_2, ffn_norm_2, ffn_w_gu_2, ffn_w_down_2,
    )


_drawn_inputs = setup_inputs


def setup_inputs(seed=0):
    import zlib

    import numpy as np

    out = dict(_drawn_inputs(seed))
    spreads = {}
    factors = {'qk_gain': 8.0,
     'pool_scale': 4.046,
     'lru_conv_b_2': 8.0,
     'lru_gate_a_b_2': 28.39,
     'lru_gate_x_b_2': 8.0,
     'mla_q_norm_2': 8.0,
     'mla_kv_norm_2': 8.0,
     'mla_qn_norm_2': 8.0,
     'mla_qr_norm_2': 8.0,
     'mla_kn_norm_2': 8.0,
     'mla_kr_norm_2': 8.0}
    for name, (base, spread) in spreads.items():
        noise = np.random.default_rng([zlib.crc32(name.encode()), seed]).standard_normal(out[name].shape)
        drawn = base * np.exp(spread * noise) if base else spread * noise
        out[name] = __import__('jax').numpy.asarray(drawn.astype(out[name].dtype))
    for name, factor in factors.items():
        out[name] = (out[name] * factor).astype(out[name].dtype)
    return out
```

```python
from contextlib import ExitStack

import concourse.bass as bass
import numpy as np
from concourse import mybir

F32 = mybir.dt.float32
I32 = mybir.dt.int32
ALU = mybir.AluOpType
ACT = mybir.ActivationFunctionType
AX_X = mybir.AxisListType.X

P = 128
S = 256
D = 1024
KT = D // P
F = 2816
FT = F // P
UC = 256
FJ = F // UC
HALF_F = FT // 2
SLOTS = 4
BANKS = 4
LAYERS1 = 2
LAYERS2 = 4
HEADS = 8
DH = 64
CHUNK = 64
N_MOD = 9
EPS = 1e-6
NEG = -1e30
MIX_COLS = 512
G_COL = 7 * MIX_COLS + HEADS
WINDOWS = (2, 4, 8, 16)
REL = 257
EXT = 384
LRU_W = 1280
LT = LRU_W // P
QL, KVL, ROPE, NOPE, VD = 384, 256, 64, 128, 128
MLA_DOWN = QL + KVL + ROPE
CQ, CKV = QL // P, KVL // P
TWO_PI = 6.283185307179586
TWO_PI_PARTS = (6.28125, 1.93500518798828125e-3, 3.0199099819e-7)
PI_BELOW = 3.1415925
ROUND = 1.5 * 2 ** 23
DVE_PER = 141

C_IDENT, C_HALVES, C_ONES, C_CAUSAL, C_INV, C_SEL, C_ROT, C_FREQ = np.cumsum(
    [0, P, P, S, S, 4 * S, HEADS * P, ROPE]).tolist()
C_EPS = C_FREQ + 1
C_ALL = C_EPS + 1

L_BADA, L_GAIN, L_QK, L_FB, L_PS, L_WF, L_WP = np.cumsum(
    [0, N_MOD * KT, 3 * KT, 4, 1, 4, KT * HEADS]).tolist()
L_ALL = L_WP + 4 * P

V_MIX, V_FFN, V_CONV, V_LCONV, V_LCB, V_LAB, V_LXB, V_LAM, V_QN, V_KVN, V_QNN, V_QRN, V_KNN, V_KRN = np.cumsum(
    [0, 4 * KT, 4 * KT, 2 * 3 * KT, 4 * LT, LT, LT, LT, LT, CQ, CKV, 1, 1, 1]).tolist()
V_ALL = V_KRN + 1


def plan_block1():
    units, g, m = [], [], []

    def ffn(n):
        for j in range(FJ):
            units.extend([("gate", n, j), ("up", n, j)])
            g.extend([("gate", n, j), ("up", n, j)])
        m.append(("mod", 2 if n == 0 else 8))
        for p in range(4):
            units.extend([("down", n, p, 0), ("down", n, p, 1)])
            g.append(("down", n, p))

    m.extend([("mod", 0), ("norm", 0)])
    ffn(0)
    m.extend([("mod", 3), ("mod", 4), ("norm", 1)])
    for u in range(2):
        units.append(("win", "u", u))
        g.append(("u", u))
    m.append("f")
    for n in range(8):
        units.append(("win", "qk", n))
        g.append(("qk", n))
        m.append(("qk", n))
    for n in range(4):
        units.append(("win", "v", n))
        g.append(("v", n))
    g.extend([("pool", 0), ("pool", 1)])
    for i in range(ATT_STEPS):
        if i < 2 * HEADS:
            m.append(("s", i))
        for what in STEP_UNITS.get(i, ()):
            units.append(what)
            g.extend([what] if what[0] == "gates" else [what + (0,), what + (1,)])
        if 0 <= i - 1 < 2 * HEADS:
            m.append(("pt", i - 1))
        if 0 <= i - 2 < 2 * HEADS:
            m.append(("pv", i - 2))
    for u in range(2):
        units.append(("branch", 2, u))
        g.extend([("branch", 2, u, 0), ("branch", 2, u, 1)])
    m.append(("mod", 5))
    for p in range(4):
        units.append(("wout", p))
        g.append(("wout", p))
    m.extend([("mod", 6), ("mod", 7), ("norm", 2)])
    ffn(1)
    return units, g, m


ATT_STEPS = 2 * HEADS + 2
STEP_UNITS = {i: [("gates", i)] for i in range(12)}
STEP_UNITS.update({12: [("branch", 1, 0)], 13: [("branch", 1, 1)], 14: [("branch", 0, 0)], 15: [("branch", 0, 1)]})


def plan_block2():
    units, g, m = [], [], []

    def plain(layer, what, n):
        for p in range(n):
            units.append((layer, what, p))
            g.append((layer, what, p))

    for layer in range(LAYERS2):
        m.append((layer, "norm", 0))
        if layer % 3 == 0:
            plain(layer, "conv", 12)
        elif layer == 1:
            plain(layer, "rec", 5)
            units.extend([(layer, "blocks", 0), (layer, "blocks", 1)])
            g.extend([(layer, "ri", t) for t in range(LT)])
            plain(layer, "gelu", 5)
        else:
            plain(layer, "cdown", 3)
            m.extend([(layer, "cq"), (layer, "ckv"), (layer, "kr"), (layer, "krot")])
            for n in range(2):
                units.append((layer, "uq", n))
                for h in range(4 * n, 4 * n + 4):
                    g.append((layer, "q", h))
                    if h >= 1:
                        m.append((layer, "qn", h - 1))
                    if h >= 2:
                        m.append((layer, "qrot", h - 2))
            units.extend([(layer, "ukv", 0), (layer, "ukv", 1)])
            g.extend([(layer, "v", n) for n in range(4)])
            m.extend([(layer, "qn", HEADS - 1), (layer, "qrot", HEADS - 2), (layer, "qrot", HEADS - 1)])
            for h in range(HEADS + 1):
                if h < HEADS:
                    g.append((layer, "k", h))
                if h >= 1:
                    m.append((layer, "kn", h - 1))
            for i in range(HEADS + 2):
                if i < HEADS:
                    m.append((layer, "s", i))
                if 0 <= i - 1 < HEADS:
                    m.append((layer, "pt", i - 1))
                if 0 <= i - 2 < HEADS:
                    m.append((layer, "pv", i - 2))
        plain(layer, "out", 4)
        m.append((layer, "norm", 1))
        for j in range(FJ):
            units.extend([(layer, "gate", j), (layer, "up", j)])
            g.extend([(layer, "gate", j), (layer, "up", j)])
        for p in range(4):
            units.extend([(layer, "down", p, 0), (layer, "down", p, 1)])
            g.append((layer, "down", p))
    return units, g, m


def build_program(nc, w, out):
    U1, G1, M1 = plan_block1()
    U2, G2, M2 = plan_block2()
    assert len(U1) % SLOTS == 0 and len(G1) % BANKS == 0 and len(M1) % BANKS == 0
    NU, NG, NM = len(U1), len(G1), len(M1)
    u_of = [{n: i for i, n in enumerate(U)} for U in (U1, U2)]
    g_of = [{n: i for i, n in enumerate(G)} for G in (G1, G2)]
    m_of = [{n: i for i, n in enumerate(M)} for M in (M1, M2)]

    def last_ticket():
        own = {}
        for b, U in enumerate((U1, U2)):
            for n in U:
                k = n[1:] if b else n
                pre = n[:1] if b else ()
                if k[0] == "down":
                    t = pre + ("down",) + ((k[1],) if b else (k[1], k[2]))
                elif k[0] == "win":
                    t = (k[1], k[2])
                elif k[0] == "branch":
                    t = n + (1,)
                elif k[0] == "blocks":
                    t = pre + ("ri", LT - 1)
                elif k[0] == "uq":
                    t = pre + ("q", 4 * k[1] + 3)
                elif k[0] == "ukv":
                    t = pre + ("k", 4 * k[1] + 3)
                elif k[0] == "wout":
                    t = n
                else:
                    t = n
                own[b, n] = g_of[b][t]
        return own

    reader = last_ticket()

    def at(l, per, n):
        return l * per + n

    with ExitStack() as ctx:
        def sb(name, shape, dt=F32):
            return ctx.enter_context(nc.sbuf_tensor(name, shape, dt))

        def sem(name):
            return ctx.enter_context(nc.semaphore(name))

        ring = sb("ring", [P, SLOTS, HALF_F * UC])
        ada_ring = sb("ada_ring", [P, 4, D])
        ada_acc = sb("ada_acc", [P, 3, D])
        x = sb("x", [P, KT, S])
        h = sb("h", [P, KT, S])
        cst = sb("cst", [P, C_ALL])
        lv = sb("lv", [P, L_ALL])
        v2 = sb("v2", [P, V_ALL])
        cact = sb("cact", [P, KT])
        mod = sb("mod", [P, N_MOD * KT])
        gains = sb("gains", [P, 3 * KT])
        qgain = sb("qgain", [P, 4])
        sqx = sb("sqx", [P, 2 * S])
        sqacc = sb("sqacc", [P, 2 * S])
        rs = sb("rs", [P, 2 * S])
        small = sb("small", [P, 24])
        lam8 = sb("lam8", [P, 2 * LT])
        lamb = sb("lamb", [P, 8, LT])
        opened = sb("opened", [P, 2 * BANKS + 1])
        posi = sb("posi", [ROPE, S], I32)
        arena = sb("arena", [P, 24320])
        taken = [0]

        def part(cols):
            taken[0] += cols
            assert taken[0] <= 24320
            return arena[:, taken[0] - cols:taken[0]]

        def tiled(ap, n):
            return ap.rearrange("p (k t) -> p k t", k=n)

        act_f = part(FT * S)
        silu_g = tiled(part(2 * 2 * S), 2)
        taken[0] = 0
        qk = tiled(part(16 * S), 16)
        vtok = part(2 * 2 * MIX_COLS).rearrange("p (a t c) -> p a t c", a=2, t=2)
        win = tiled(part(8 * S), 2)
        taken[0] -= 8 * S
        logit = tiled(part(2 * 3 * P), 2)
        prob = tiled(part(2 * 3 * P), 2)
        part(2 * S)
        u_in = part(4 * S)
        gates = tiled(part(24 * S), 24)
        relb = tiled(part(HEADS * S), HEADS)
        ybr = tiled(part(12 * S), 12)
        probT = tiled(part(2 * 3 * P), 2)
        sqb = tiled(part(2 * 2 * S), 2)
        fz = tiled(part(8 * S), 8)
        taken[0] = 0
        cv_c = tiled(part(KT * S), KT)
        cv_o = tiled(part(KT * S), KT)
        mix_y = tiled(part(KT * S), KT)
        taken[0] = 0
        r_raw, r_rec, r_r, r_i, r_a, r_t, r_g = (tiled(part(LT * S), LT) for _ in range(7))
        taken[0] = 0
        c_lat = tiled(part(6 * S), 6)
        c_sq = tiled(part(6 * S), 6)
        qn = tiled(part(HEADS * S), HEADS)
        qr = tiled(part(HEADS * S), HEADS)
        kn = tiled(part(HEADS * S), HEADS)
        mla_y = tiled(part(HEADS * S), HEADS)
        mla_v = tiled(part(2 * D), 2)
        cosT, sinT, rope_a, rope_b, rope_c = (part(S) for _ in range(5))
        hsq = tiled(part(2 * 2 * S), 2)
        lroot = tiled(part(3 * S), 3)
        m_logit, m_prob, m_probT = (tiled(part(2 * 3 * P), 2) for _ in range(3))

        ident = cst[:, C_IDENT:C_IDENT + P]
        halves = cst[:, C_HALVES:C_HALVES + P]
        ones = cst[:, C_ONES:C_ONES + P]
        ones_row = cst[:, C_ONES:C_ONES + S]
        causal = cst[:, C_CAUSAL:C_CAUSAL + S]
        inv_count = tiled(cst[:, C_INV:C_INV + 4 * S], 4)
        eps = cst[:, C_EPS:C_EPS + 1]

        psum = [ctx.enter_context(nc.psum_tensor(f"ps{b}", [P, 2 * S], F32)) for b in range(2 * BANKS)]

        def gbank(t):
            return psum[t % BANKS]

        def mbank(t):
            return psum[BANKS + t % BANKS]

        def two(bank):
            return bank[:, :].rearrange("p (t s) -> p t s", t=2)

        rel_rows = nc.dram_tensor("rel_rows", [LAYERS1 * HEADS, EXT], F32, kind="Internal")

        unit_loaded = [sem(f"unit_loaded{s}") for s in range(SLOTS)]
        g_full = sem("g_full")
        m_full = sem("m_full")
        g_free = [sem(f"g_free{b}") for b in range(BANKS)]
        m_free = [sem(f"m_free{b}") for b in range(BANKS)]
        const_loaded = sem("const_loaded")
        x_loaded = sem("x_loaded")
        c_loaded = sem("c_loaded")
        rel_loaded = sem("rel_loaded")
        rel_padded = sem("rel_padded")
        rel_stored = sem("rel_stored")
        relb_loaded = sem("relb_loaded")
        relb_masked = sem("relb_masked")
        lv_loaded = sem("lv_loaded")
        pos_loaded = sem("pos_loaded")
        cact_ready = sem("cact_ready")
        ada_loaded = [sem(f"ada_loaded{s}") for s in range(4)]
        ada_step = sem("ada_step")
        dve_step = sem("dve_step")
        x_ready = sem("x_ready")
        h_scaled = sem("h_scaled")
        h_ready = sem("h_ready")
        diff_ready = sem("diff_ready")
        qk_ready = sem("qk_ready")
        f_abs = sem("f_abs")
        f_exp = sem("f_exp")
        decay_ready = sem("decay_ready")
        max_ready = sem("max_ready")
        exp_ready = sem("exp_ready")
        prob_ready = sem("prob_ready")
        merged_ready = sem("merged_ready")
        mix_ready = sem("mix_ready")
        lam_abs = sem("lam_abs")
        lam_exp = sem("lam_exp")
        lam_ready = sem("lam_ready")
        sig_ready = sem("sig_ready")
        decay_exp = sem("decay_exp")
        var_ready = sem("var_ready")
        var_root = sem("var_root")
        angle_ready = sem("angle_ready")
        sincos_ready = sem("sincos_ready")
        lat_ready = sem("lat_ready")
        head_ready = sem("head_ready")
        rope_ready = sem("rope_ready")
        stored = sem("stored")

        NORMS = 3

        wg = w["ffn_w_gate"].rearrange("l j (k p) f -> l j p k f", p=P)
        wu = w["ffn_w_up"].rearrange("l j (k p) f -> l j p k f", p=P)
        wd = w["ffn_w_down"].rearrange("l j (k p) d -> l j p k d", p=P)
        w_in = w["w_in"].rearrange("l (k p) n -> l p k n", p=P)
        w_br = w["w_branch"].rearrange("l b (k p) d -> l b p k d", p=P)
        w_out = w["w_out"].rearrange("l (k p) d -> l p k d", p=P)
        w_ada = w["w_ada"].rearrange("l (k p) n -> l p k n", p=P)
        cw_in = w["conv_w_in_2"].rearrange("l (k p) n -> l p k n", p=P)
        cw_out = w["conv_w_out_2"].rearrange("l (k p) n -> l p k n", p=P)
        rw_in = w["lru_w_in_2"].rearrange("l (k p) n -> l p k n", p=P)
        rw_out = w["lru_w_out_2"].rearrange("l (k p) n -> l p k n", p=P)
        rw_a = w["lru_gate_a_w_2"].rearrange("l n d e -> l d n e")
        rw_x = w["lru_gate_x_w_2"].rearrange("l n d e -> l d n e")
        mw_down = w["mla_w_down_2"].rearrange("l (k p) n -> l p k n", p=P)
        mw_uq = w["mla_w_uq_2"].rearrange("l (k p) n -> l p k n", p=P)
        mw_ukv = w["mla_w_ukv_2"].rearrange("l (k p) n -> l p k n", p=P)
        mw_o = w["mla_w_o_2"].rearrange("l (k p) n -> l p k n", p=P)
        w_gu = w["ffn_w_gu_2"].rearrange("l (k p) n -> l p k n", p=P)
        w_dn = w["ffn_w_down_2"].rearrange("l (k p) n -> l p k n", p=P)

        WIN_COL = {"u": lambda n: 3 * MIX_COLS + UC * n,
                   "qk": lambda n: (0 if n < 4 else 4 * MIX_COLS) + UC * (n % 4),
                   "v": lambda n: (2 * MIX_COLS if n < 2 else 6 * MIX_COLS) + UC * (n % 2)}

        def slot(u, nk, cols):
            return ring[:, u % SLOTS, 0:nk * cols].rearrange("p (k c) -> p k c", k=nk)

        def ada_count(l, j, k):
            return at(l, N_MOD * (2 * KT - 1), (2 * KT - 1) * j + 1 + 2 * k)

        def g_taken(eng, b, l, name):
            t = g_of[b][name]
            eng.wait_ge(g_free[t % BANKS], at(l, NG // BANKS, t // BANKS + 1) + 1)

        def m_taken(eng, b, l, name):
            t = m_of[b][name]
            eng.wait_ge(m_free[t % BANKS], at(l, NM // BANKS, t // BANKS + 1) + 1)

        block = ctx.enter_context(nc.Block())

        @block.sync
        def _(sp):
            def load(b, l, name, src):
                u = u_of[b][name]
                if u >= SLOTS:
                    sp.wait_ge(g_full, at(l, NG, reader[b, (U2 if b else U1)[u - SLOTS]] + 1) + 1)
                else:
                    sp.wait_ge(g_full, at(l, NG, 0) + 1)
                sp.dma_start(slot(u, src.shape[1], src.shape[2]), src).then_inc(unit_loaded[u % SLOTS], 16)

            def load_ffn(b, l, gate0, gate, up, down):
                g0 = g_of[b][gate0]
                u0 = u_of[b][gate0]
                name = (lambda what, j: gate0[:1] + (what, j)) if b else (lambda what, j: (what, gate0[1], j))
                load(b, l, name("gate", 0), gate(0))
                load(b, l, name("up", 0), up(0))
                with sp.Fori(0, (FJ - 1) // 2) as i:
                    for s in range(4):
                        u = u0 + 2 + s
                        j = sp.snap(2 * i + 1 + s // 2)
                        sp.wait_ge(g_full, at(l, NG, max(g0 + s - 1, 0)) + 4 * i + 1)
                        src = (gate, up)[s % 2](j)
                        sp.dma_start(slot(u, KT, UC), src).then_inc(unit_loaded[u % SLOTS], 16)
                for p in range(4):
                    for half in range(2):
                        n = gate0[:1] + ("down", p, half) if b else ("down", gate0[1], p, half)
                        load(b, l, n, down(p, half))

            def cols(n):
                return bass.ds(UC * n, UC)

            def ffn1(l, n):
                load_ffn(0, l, ("gate", n, 0), lambda j: wg[l, n, :, :, cols(j)], lambda j: wu[l, n, :, :, cols(j)],
                         lambda p, half: wd[l, n, :, half * HALF_F:(half + 1) * HALF_F, UC * p:UC * (p + 1)])

            with sp.Fori(0, LAYERS1) as l:
                ffn1(l, 0)
                w_in_tiles = w["w_in"].rearrange("l (k p) n -> p (l k) n", p=P)
                w_br_tiles = w["w_branch"].rearrange("l b (k p) d -> p (l b k) d", p=P)
                for n in U1[u_of[0][("win", "u", 0)]:u_of[0][("gate", 1, 0)]]:
                    if n[0] == "win":
                        c = WIN_COL[n[1]](n[2])
                        src = w_in[l, :, :, c:c + UC] if c else w_in_tiles[:, bass.ds(l * KT, KT), 0:UC]
                    elif n[0] == "gates":
                        src = w_in[l, :, :, G_COL + UC * n[1]:G_COL + UC * (n[1] + 1)]
                    elif n[0] == "branch":
                        src = w_br[l, n[1], :, :, 2 * UC * n[2]:2 * UC * (n[2] + 1)]
                        if n[1:] == (0, 0):
                            src = w_br_tiles[:, bass.ds(l * 3 * (MIX_COLS // P), MIX_COLS // P), 0:2 * UC]
                    else:
                        src = w_out[l, :, :, UC * n[1]:UC * (n[1] + 1)]
                    load(0, l, n, src)
                ffn1(l, 1)

            L2 = LAYERS1
            for layer in range(LAYERS2):
                for n in U2:
                    if n[0] != layer or n[1] in ("gate", "up", "down"):
                        continue
                    if n[1] == "conv":
                        c = (D * (1 + n[2] // 4)) % (3 * D) + UC * (n[2] % 4)
                        src = cw_in[layer // 3, :, :, c:c + UC]
                    elif n[1] == "rec":
                        src = rw_in[0, :, :, LRU_W + UC * n[2]:LRU_W + UC * (n[2] + 1)]
                    elif n[1] == "gelu":
                        src = rw_in[0, :, :, UC * n[2]:UC * (n[2] + 1)]
                    elif n[1] == "blocks":
                        src = (rw_a, rw_x)[n[2]][0]
                    elif n[1] == "cdown":
                        src = mw_down[0, :, :, UC * n[2]:min(UC * (n[2] + 1), QL + KVL + ROPE)]
                    elif n[1] == "uq":
                        src = mw_uq[0, :, :, 768 * n[2]:768 * (n[2] + 1)]
                    elif n[1] == "ukv":
                        src = mw_ukv[0, :, :, D * n[2]:D * (n[2] + 1)]
                    else:
                        o = (cw_out[layer // 3], rw_out[0], mw_o[0])[layer % 3]
                        src = o[:, :, UC * n[2]:UC * (n[2] + 1)]
                    load(1, L2, n, src)
                load_ffn(1, L2, (layer, "gate", 0), lambda j: w_gu[layer, :, :, cols(j)],
                         lambda j: w_gu[layer, :, :, bass.ds(UC * j + F, UC)],
                         lambda p, half: w_dn[layer, :, half * HALF_F:(half + 1) * HALF_F, UC * p:UC * (p + 1)])

            for p in range(4):
                g_taken(sp, 1, L2, (LAYERS2 - 1, "down", p))
                sp.dma_start(out[:, 2 * p:2 * p + 2, :], x[:, 2 * p:2 * p + 2, :]).then_inc(stored, 16)
            sp.wait_ge(stored, 64)

        @block.gpsimd
        def _(pool):
            pool.wait_ge(cact_ready, 1)

            def row_free(l, j):
                m_taken(pool, 0, l, ("mod", 0 if j == 1 else j))

            with pool.Fori(0, LAYERS1) as l:
                for j in range(N_MOD):
                    def fetch(k):
                        src = w_ada[l, :, k, D * j:D * (j + 1)]
                        pool.dma_start(ada_ring[:, k % 4, :], src).then_inc(ada_loaded[k % 4], 16)

                    for k in range(4):
                        fetch(k)
                    if j >= 3:
                        row_free(l, j - 3)
                    acc = ada_acc[:, j % 3, :]
                    for k in range(KT):
                        rows = ada_ring[:, k % 4, :]
                        scale = cact[:, k:k + 1].to_broadcast([P, D])
                        pool.wait_ge(ada_loaded[k % 4], at(l, 16 * 2 * N_MOD, 16 * (2 * j + k // 4 + 1)))
                        pool.tensor_tensor(rows if k else acc, rows, scale, ALU.mult).then_inc(ada_step, 1)
                        if k:
                            pool.wait_ge(ada_step, ada_count(l, j, k) - 1)
                            pool.tensor_tensor(acc, acc, rows, ALU.add).then_inc(ada_step, 1)
                        if k < 4:
                            pool.wait_ge(ada_step, ada_count(l, j, k))
                            fetch(k + 4)
                    pool.wait_ge(ada_step, ada_count(l, j, KT - 1))
                for j in range(6, N_MOD):
                    row_free(l, j)

        @block.tensor
        def _(pe):
            def open_g(b, l, name):
                t = g_of[b][name]
                pe.wait_ge(g_free[t % BANKS], at(l, NG // BANKS, t // BANKS) + 1)
                return gbank(t)

            def open_m(b, l, name):
                t = m_of[b][name]
                pe.wait_ge(m_free[t % BANKS], at(l, NM // BANKS, t // BANKS) + 1)
                return mbank(t)

            def unit(b, l, name, nk, cols):
                u = u_of[b][name]
                pe.wait_ge(unit_loaded[u % SLOTS], at(l, 16 * NU // SLOTS, 16 * (u // SLOTS + 1)))
                return slot(u, nk, cols)

            def tiles(bank, wt, rhs, n, hwait=None):
                nk = wt.shape[1]
                for t in range(n):
                    for k in range(nk):
                        if hwait and t == 0:
                            hwait(k)
                        mm = pe.matmul(two(bank)[:, t, :], wt[:, k, P * t:P * (t + 1)], rhs[:, k, :],
                                       start=(k == 0), stop=(k == nk - 1))
                return mm

            def mod_row(l, rows):
                bank = open_m(0, l, ("mod", rows[0]))
                for n, j in enumerate(rows):
                    pe.wait_ge(ada_step, ada_count(l, j, KT - 1))
                    for c in range(KT):
                        mm = pe.matmul(bank[:, KT * n + c:KT * n + c + 1], ada_acc[:, j % 3, P * c:P * (c + 1)],
                                       ones[:, 0:1], start=True, stop=True)
                mm.then_inc(m_full, 1)

            def norm_sum(b, l, name, nn):
                bank = open_m(b, l, name)
                pe.wait_ge(x_ready, (nn + 1) * 4)
                for t in range(2):
                    mm = pe.matmul(bank[:, 0:S], ones, sqacc[:, S * t:S * (t + 1)], start=(t == 0), stop=(t == 1))
                mm.then_inc(m_full, 1)

            def h_tile(nn):
                return lambda k: pe.wait_ge(h_ready, nn * KT + k + 1)

            def ffn(b, l, gate0, nn, between=None):
                g0, u0 = g_of[b][gate0], u_of[b][gate0]
                up0 = (gate0[0], "up", 0) if b else ("up", gate0[1], 0)
                for name, hw in ((gate0, h_tile(nn)), (up0, None)):
                    wt = unit(b, l, name, KT, UC)
                    tiles(open_g(b, l, name), wt, h, 2, hw).then_inc(g_full, 1)
                with pe.Fori(0, (FJ - 1) // 2) as i:
                    for s in range(4):
                        u, g = u0 + 2 + s, g0 + 2 + s
                        pe.wait_ge(unit_loaded[u % SLOTS], at(l, 16 * NU // SLOTS, 16 * (u // SLOTS + 1)) + 16 * i)
                        pe.wait_ge(g_free[g % BANKS], at(l, NG // BANKS, g // BANKS) + i + 1)
                        tiles(gbank(g), slot(u, KT, UC), h, 2).then_inc(g_full, 1)
                if between:
                    between()
                act = tiled(act_f, FT)
                for p in range(4):
                    down = (gate0[0], "down", p) if b else ("down", gate0[1], p)
                    bank = two(open_g(b, l, down))
                    for half in range(2):
                        wt = unit(b, l, down + (half,), HALF_F, UC)
                        if p == 0:
                            g_taken(pe, b, l, up0[:-1] + ((HALF_F // 2, FJ - 1)[half],))
                        for t in range(2):
                            for k in range(HALF_F):
                                mm = pe.matmul(bank[:, t, :], wt[:, k, P * t:P * (t + 1)],
                                               act[:, half * HALF_F + k, :], start=(half == 0 and t == 0 and k == 0),
                                               stop=(half == 1 and k == HALF_F - 1), skip_group_check=True)
                    mm.then_inc(g_full, 1)

            def qk_sum(l, n):
                bank = open_m(0, l, ("qk", n))
                g_taken(pe, 0, l, ("qk", n))
                pe.matmul(bank[:, :], halves, sqb[:, n % 2, :], start=True, stop=True).then_inc(m_full, 1)

            def scores(l, s):
                a, hd = s // HEADS, s % HEADS
                rows = slice(DH * (hd % 2), DH * (hd % 2) + DH)
                q, k = qk[rows, 8 * a + hd // 2, :], qk[rows, 8 * a + 4 + hd // 2, :]
                bank = open_m(0, l, ("s", s))
                pe.wait_ge(qk_ready, at(l, 8, 4 * a + 3 + (hd // 2) // 2))
                for lo, hi, keys in ((0, P, P), (P, 3 * P, S)):
                    mm = pe.matmul(bank[:, lo:hi], q[:, 0:P] if lo == 0 else q[:, P:S], k[:, 0:keys],
                                   start=True, stop=(a == 0))
                    if a:
                        if lo == 0 and hd == 0:
                            pe.wait_ge(decay_ready, at(l, 1, 1))
                        mm = pe.matmul(bank[:, lo:hi], cst[0:HEADS, C_SEL + P * hd:C_SEL + P * (hd + 1)],
                                       fz[0:HEADS, 0, 0:keys], start=False, stop=True)
                mm.then_inc(m_full, 1)

            def turn_probs(b, l, name, n, pr):
                bank = open_m(b, l, name)
                pe.wait_ge(prob_ready, n + 1)
                for i in range(3):
                    mm = pe.transpose(bank[:, P * i:P * (i + 1)], pr[:, P * i:P * (i + 1)], ident)
                mm.then_inc(m_full, 1)

            def values(b, l, name, turned, v0, v1, rows, pt):
                bank = open_m(b, l, name)
                m_taken(pe, b, l, turned)
                pe.matmul(bank[rows, 0:S], v0, pt[:, 0:S], start=True, stop=False)
                pe.matmul(bank[rows, P:S], v1, pt[:, S:3 * P], start=False, stop=True).then_inc(m_full, 1)

            def branch(l, n, u):
                wt = unit(0, l, ("branch", n, u), 4, 2 * UC)
                for i in range(2):
                    bank = open_g(0, l, ("branch", n, u, i))
                    tiles(bank, wt[:, :, UC * i:UC * (i + 1)], ybr[:, 4 * n:4 * n + 4, :], 2).then_inc(g_full, 1)

            pe.wait_ge(const_loaded, 32)
            with pe.Fori(0, LAYERS1) as l:
                mod_row(l, [0, 1])
                norm_sum(0, l, ("norm", 0), l * NORMS)
                ffn(0, l, ("gate", 0, 0), l * NORMS, lambda: mod_row(l, [2]))
                mod_row(l, [3])
                mod_row(l, [4])
                norm_sum(0, l, ("norm", 1), l * NORMS + 1)
                for u in range(2):
                    wt = unit(0, l, ("win", "u", u), KT, UC)
                    tiles(open_g(0, l, ("u", u)), wt, h, 2, None if u else h_tile(l * NORMS + 1)).then_inc(g_full, 1)
                bank = open_m(0, l, "f")
                for k in range(KT):
                    mm = pe.matmul(bank[0:HEADS, 0:S], lv[:, L_WF + HEADS * k:L_WF + HEADS * (k + 1)], h[:, k, :],
                                   start=(k == 0), stop=(k == KT - 1))
                mm.then_inc(m_full, 1)
                for n in range(8):
                    wt = unit(0, l, ("win", "qk", n), KT, UC)
                    tiles(open_g(0, l, ("qk", n)), wt, h, 2).then_inc(g_full, 1)
                    if n:
                        qk_sum(l, n - 1)
                for n in range(4):
                    wt = unit(0, l, ("win", "v", n), KT, UC)
                    bank = two(open_g(0, l, ("v", n)))
                    for t in range(2):
                        for k in range(KT):
                            mm = pe.matmul(bank[:, t, :], h[:, k, P * t:P * (t + 1)], wt[:, k, :],
                                           start=(k == 0), stop=(k == KT - 1))
                    mm.then_inc(g_full, 1)
                    if n == 0:
                        qk_sum(l, 7)
                for n in range(2):
                    bank = two(open_g(0, l, ("pool", n)))
                    pe.wait_ge(diff_ready, at(l, 1, 1))
                    for t in range(2):
                        c = 2 * n + t
                        mm = pe.matmul(bank[:, t, :], lv[:, L_WP + P * c:L_WP + P * (c + 1)],
                                       win[:, 1, S * c:S * (c + 1)], start=True, stop=True)
                    mm.then_inc(g_full, 1)
                for i in range(ATT_STEPS):
                    if i < 2 * HEADS:
                        scores(l, i)
                    for what in STEP_UNITS.get(i, ()):
                        if what[0] == "gates":
                            wt = unit(0, l, what, KT, UC)
                            tiles(open_g(0, l, what), wt, h, 2).then_inc(g_full, 1)
                        else:
                            if what == ("branch", 1, 0):
                                g_taken(pe, 0, l, ("pool", 1))
                            if what == ("branch", 0, 0):
                                m_taken(pe, 0, l, ("pv", HEADS - 1))
                            branch(l, what[1], what[2])
                    if 0 <= i - 1 < 2 * HEADS:
                        turn_probs(0, l, ("pt", i - 1), at(l, 2 * HEADS, i - 1), prob[:, (i - 1) % 2, :])
                    if 0 <= i - 2 < 2 * HEADS:
                        s = i - 2
                        if s == 0:
                            g_taken(pe, 0, l, ("v", 3))
                        a, hd = s // HEADS, s % HEADS
                        c = slice(DH * hd, DH * (hd + 1))
                        values(0, l, ("pv", s), ("pt", s), vtok[:, a, 0, c], vtok[:, a, 1, c],
                               slice(DH * (hd % 2), DH * (hd % 2) + DH), probT[:, s % 2, :])
                m_taken(pe, 0, l, ("pv", 2 * HEADS - 1))
                for u in range(2):
                    branch(l, 2, u)
                mod_row(l, [5])
                for p in range(4):
                    wt = unit(0, l, ("wout", p), KT, UC)
                    bank = open_g(0, l, ("wout", p))
                    hw = None if p else (lambda k: pe.wait_ge(merged_ready, at(l, 4, k // 2 + 1)))
                    tiles(bank, wt, h, 2, hw).then_inc(g_full, 1)
                mod_row(l, [6])
                mod_row(l, [7])
                norm_sum(0, l, ("norm", 2), l * NORMS + 2)
                ffn(0, l, ("gate", 1, 0), l * NORMS + 2, lambda: mod_row(l, [8]))

            L2 = LAYERS1
            for layer in range(LAYERS2):
                nn = NORMS * LAYERS1 + 2 * layer
                norm_sum(1, L2, (layer, "norm", 0), nn)
                first = [h_tile(nn)]

                def plain(what, n):
                    for p in range(n):
                        wt = unit(1, L2, (layer, what, p), KT, UC)
                        tiles(open_g(1, L2, (layer, what, p)), wt, h, 2, first.pop() if first else None)\
                            .then_inc(g_full, 1)

                if layer % 3 == 0:
                    plain("conv", 12)
                    y, nk = mix_y, KT
                elif layer == 1:
                    plain("rec", 5)
                    wa = unit(1, L2, (1, "blocks", 0), LT, P)
                    wx = unit(1, L2, (1, "blocks", 1), LT, P)
                    for t in range(LT):
                        bank = two(open_g(1, L2, (1, "ri", t)))
                        pe.wait_ge(mix_ready, t + 1)
                        pe.matmul(bank[:, 0, :], wa[:, t, :], r_rec[:, t, :], start=True, stop=True)
                        pe.matmul(bank[:, 1, :], wx[:, t, :], r_rec[:, t, :], start=True, stop=True)\
                            .then_inc(g_full, 1)
                    plain("gelu", 5)
                    y, nk = r_g, LT
                else:
                    for p in range(3):
                        cols = UC if p < 2 else P + ROPE
                        wt = unit(1, L2, (2, "cdown", p), KT, cols)
                        bank = two(open_g(1, L2, (2, "cdown", p)))
                        hw = first.pop() if first else None
                        for t in range(2):
                            n = P if 2 * p + t < 5 else ROPE
                            for k in range(KT):
                                if hw and t == 0:
                                    hw(k)
                                mm = pe.matmul(bank[0:n, t, :], wt[:, k, P * t:P * t + n], h[:, k, :],
                                               start=(k == 0), stop=(k == KT - 1))
                        mm.then_inc(g_full, 1)
                    for name, lo, n, p, last in (("cq", 0, CQ, P, 1), ("ckv", CQ, CKV, P, 2), ("kr", 5, 1, ROPE, 2)):
                        bank = open_m(1, L2, (2, name))
                        g_taken(pe, 1, L2, (2, "cdown", last))
                        for k in range(n):
                            mm = pe.matmul(bank[0:p, 0:S], ones[0:p, 0:p], c_sq[0:p, lo + k, :],
                                           start=(k == 0), stop=(k == n - 1))
                        mm.then_inc(m_full, 1)
                    bank = open_m(1, L2, (2, "krot"))
                    pe.wait_ge(lat_ready, 3)
                    pe.matmul(bank[0:ROPE, 0:S], cst[0:ROPE, C_ROT:C_ROT + ROPE], c_lat[0:ROPE, 5, :],
                              start=True, stop=True).then_inc(m_full, 1)

                    def q_sum(hd):
                        bank = open_m(1, L2, (2, "qn", hd))
                        g_taken(pe, 1, L2, (2, "q", hd))
                        pe.matmul(bank[:, 0:S], ones, hsq[:, hd % 2, 0:S], start=True, stop=True)
                        pe.matmul(bank[0:ROPE, S:2 * S], ones[0:ROPE, 0:ROPE], hsq[0:ROPE, hd % 2, S:2 * S],
                                  start=True, stop=True).then_inc(m_full, 1)

                    def q_rot(hd):
                        bank = open_m(1, L2, (2, "qrot", hd))
                        pe.wait_ge(head_ready, hd + 1)
                        pe.matmul(bank[0:ROPE, 0:S], cst[0:ROPE, C_ROT:C_ROT + ROPE], qr[0:ROPE, hd, :],
                                  start=True, stop=True).then_inc(m_full, 1)

                    pe.wait_ge(lat_ready, 3)
                    for hd in range(HEADS):
                        wt = unit(1, L2, (2, "uq", hd // 4), CQ, 768)
                        bank = two(open_g(1, L2, (2, "q", hd)))
                        c = (NOPE + ROPE) * (hd % 4)
                        for t, (lo, n) in enumerate(((c, NOPE), (c + NOPE, ROPE))):
                            for k in range(CQ):
                                mm = pe.matmul(bank[0:n, t, :], wt[:, k, lo:lo + n], c_lat[:, k, :],
                                               start=(k == 0), stop=(k == CQ - 1))
                        mm.then_inc(g_full, 1)
                        if hd >= 1:
                            q_sum(hd - 1)
                        if hd >= 2:
                            q_rot(hd - 2)
                    wkv = [unit(1, L2, (2, "ukv", n), CKV, D) for n in range(2)]
                    for n in range(4):
                        t, grp = n % 2, n // 2
                        bank = open_g(1, L2, (2, "v", n))
                        for k in range(CKV):
                            vw = wkv[grp][:, k, :].rearrange("p (a c) -> p a c", a=4)[:, :, NOPE:NOPE + VD]
                            mm = pe.matmul(bank[:, :], c_lat[:, CQ + k, P * t:P * (t + 1)], vw,
                                           start=(k == 0), stop=(k == CKV - 1))
                        mm.then_inc(g_full, 1)
                    q_sum(HEADS - 1)
                    q_rot(HEADS - 2)
                    q_rot(HEADS - 1)
                    for hd in range(HEADS + 1):
                        if hd < HEADS:
                            bank = open_g(1, L2, (2, "k", hd))
                            for k in range(CKV):
                                lo = (NOPE + VD) * (hd % 4)
                                mm = pe.matmul(bank[:, 0:S], wkv[hd // 4][:, k, lo:lo + NOPE], c_lat[:, CQ + k, :],
                                               start=(k == 0), stop=(k == CKV - 1))
                            mm.then_inc(g_full, 1)
                        if hd >= 1:
                            bank = open_m(1, L2, (2, "kn", hd - 1))
                            g_taken(pe, 1, L2, (2, "k", hd - 1))
                            pe.matmul(bank[:, 0:S], ones, hsq[:, (hd - 1) % 2, 0:S], start=True, stop=True)\
                                .then_inc(m_full, 1)
                    pe.wait_ge(rope_ready, HEADS + 1)
                    for i in range(HEADS + 2):
                        if i < HEADS:
                            bank = open_m(1, L2, (2, "s", i))
                            pe.wait_ge(head_ready, HEADS + i + 1)
                            for lo, hi, keys in ((0, P, P), (P, 3 * P, S)):
                                qs = slice(0, P) if lo == 0 else slice(P, S)
                                pe.matmul(bank[:, lo:hi], qn[:, i, qs], kn[:, i, 0:keys], start=True, stop=False)
                                mm = pe.matmul(bank[:, lo:hi], qr[0:ROPE, i, qs], c_lat[0:ROPE, 5, 0:keys],
                                               start=False, stop=True)
                            mm.then_inc(m_full, 1)
                        if 0 <= i - 1 < HEADS:
                            turn_probs(1, L2, (2, "pt", i - 1), LAYERS1 * 2 * HEADS + i - 1, m_prob[:, (i - 1) % 2, :])
                        if 0 <= i - 2 < HEADS:
                            hd = i - 2
                            if hd == 0:
                                g_taken(pe, 1, L2, (2, "v", 3))
                            c = slice(VD * hd, VD * (hd + 1))
                            values(1, L2, (2, "pv", hd), (2, "pt", hd), mla_v[:, 0, c], mla_v[:, 1, c],
                                   slice(0, P), m_probT[:, hd % 2, :])
                    y, nk = mla_y, KT

                for p in range(4):
                    wt = unit(1, L2, (layer, "out", p), nk, UC)
                    bank = open_g(1, L2, (layer, "out", p))
                    if layer % 3 == 0:
                        hw = lambda k: g_taken(pe, 1, L2, (layer, "conv", 8 + k // 2))
                    elif layer == 1:
                        hw = lambda k: pe.wait_ge(mix_ready, LT + k + 1)
                    else:
                        hw = lambda k: m_taken(pe, 1, L2, (2, "pv", k))
                    tiles(bank, wt, y, 2, None if p else hw).then_inc(g_full, 1)
                norm_sum(1, L2, (layer, "norm", 1), nn + 1)
                ffn(1, L2, (layer, "gate", 0), nn + 1)

        @block.scalar
        def _(act):
            def g_full_at(b, l, name):
                t = g_of[b][name]
                act.wait_ge(g_full, at(l, NG, t + 1) + 1)
                return gbank(t), g_free[t % BANKS]

            def m_full_at(b, l, name):
                t = m_of[b][name]
                act.wait_ge(m_full, at(l, NM, t + 1))
                return mbank(t), m_free[t % BANKS]

            def root(b, l, name):
                bank, free = m_full_at(b, l, name)
                act.activation(rs[:, 0:S], bank[:, 0:S], ACT.Sqrt, bias=eps, scale=1.0 / D).then_inc(free, 1)

            def add_shift(l, n, row):
                for k in range(KT):
                    act.wait_ge(h_scaled, (l * NORMS + n) * KT + k + 1)
                    act.activation(h[:, k, :], h[:, k, :], ACT.Identity,
                                   bias=mod[:, KT * row + k:KT * row + k + 1]).then_inc(h_ready, 1)

            def silus(b, l, gate0):
                g0 = g_of[b][gate0]
                bank, free = g_full_at(b, l, gate0)
                act.activation(silu_g[:, 0, :], bank[:, :], ACT.Silu).then_inc(free, 1)
                with act.Fori(0, (FJ - 1) // 2) as i:
                    for s in range(2):
                        g = g0 + 2 + 2 * s
                        act.wait_ge(g_full, at(l, NG, g + 1) + 4 * i + 1)
                        act.wait_ge(g_free[(g - 3) % BANKS], at(l, NG // BANKS, (g - 3) // BANKS + 1) + i + 1)
                        act.activation(silu_g[:, (1 + s) % 2, :], gbank(g)[:, :], ACT.Silu)\
                            .then_inc(g_free[g % BANKS], 1)

            def exps(count, lg, pr, used):
                n, s = count
                act.wait_ge(max_ready, n + 1)
                if used is not None:
                    act.wait_ge(m_full, used)
                act.activation(pr[:, s, 0:P], lg[:, s, 0:P], ACT.Exp, bias=small[:, 6 * s:6 * s + 1],
                               accum_out=small[:, 6 * s + 2:6 * s + 3])
                act.activation(pr[:, s, P:3 * P], lg[:, s, P:3 * P], ACT.Exp, bias=small[:, 6 * s + 1:6 * s + 2],
                               accum_out=small[:, 6 * s + 3:6 * s + 4]).then_inc(exp_ready, 1)

            def copy_turned(b, l, i, pre, pt):
                bank, free = m_full_at(b, l, pre + ("pt", i))
                if i >= 2:
                    act.wait_ge(m_full, at(l, NM, m_of[b][pre + ("pv", i - 2)] + 1))
                act.activation(pt[:, i % 2, :], bank[:, 0:3 * P], ACT.Copy).then_inc(free, 1)

            act.dma_start(x[:, :, :], w["x"]).then_inc(x_loaded, 16)
            act.dma_start(cact[:, :], w["c"]).then_inc(c_loaded, 16)
            act.dma_start(cst[:, :], w["constants"]).then_inc(const_loaded, 16)
            act.dma_start(v2[:, :], w["vectors_2"]).then_inc(const_loaded, 16)
            act.dma_start(arena[0:LAYERS1 * HEADS, 0:REL - 1],
                          w["rel_bias"].rearrange("l h r -> (l h) r")[:, 1:REL]).then_inc(rel_loaded, 16)
            act.dma_start(posi[:, :], w["positions_2"].partition_broadcast(ROPE)).then_inc(pos_loaded, 16)
            act.wait_ge(c_loaded, 16)
            act.activation(cact[:, :], cact[:, :], ACT.Silu).then_inc(cact_ready, 1)
            act.wait_ge(rel_padded, 1)
            act.dma_start(rel_rows[:, :], arena[0:LAYERS1 * HEADS, 0:EXT]).then_inc(rel_stored, 16)
            act.wait_ge(rel_stored, 16)
            act.wait_ge(const_loaded, 32)

            with act.Fori(0, LAYERS1) as l:
                act.wait_ge(x_ready, at(l, 12, 4))
                act.dma_start(lv[:, :], w["vectors_1"][l]).then_inc(lv_loaded, 16)
                root(0, l, ("norm", 0))
                add_shift(l, 0, 0)
                silus(0, l, ("gate", 0, 0))
                root(0, l, ("norm", 1))
                act.dma_start(relb[:, :, :], bass.AP(rel_rows, l * (HEADS * EXT), [[1, P], [EXT, HEADS], [1, S]]))\
                    .then_inc(relb_loaded, 16)
                add_shift(l, 1, 3)
                for u in range(2):
                    bank, free = g_full_at(0, l, ("u", u))
                    act.activation(u_in[:, 2 * S * u:2 * S * (u + 1)], bank[:, :], ACT.Copy).then_inc(free, 1)

                def qk_root_of(n):
                    bank, free = m_full_at(0, l, ("qk", n))
                    act.activation(sqb[:, n % 2, :], bank[:, :], ACT.Sqrt, bias=eps, scale=1.0 / DH).then_inc(free, 1)

                for n in range(8):
                    bank, free = g_full_at(0, l, ("qk", n))
                    if n >= 2:
                        act.wait_ge(qk_ready, at(l, 8, n - 1))
                    act.activation(qk[:, 2 * n:2 * n + 2, :], two(bank), ACT.Copy)
                    act.activation(sqb[:, n % 2, :], bank[:, :], ACT.Square).then_inc(free, 1)
                    if n == 0:
                        act.wait_ge(f_abs, at(l, 1, 1))
                        act.activation(fz[0:HEADS, 3, :], fz[0:HEADS, 2, :], ACT.Exp, scale=-1.0).then_inc(f_exp, 1)
                    else:
                        qk_root_of(n - 1)
                for n in range(4):
                    bank, free = g_full_at(0, l, ("v", n))
                    act.activation(vtok[:, n // 2, :, UC * (n % 2):UC * (n % 2 + 1)], two(bank), ACT.Copy)\
                        .then_inc(free, 1)
                    if n == 0:
                        qk_root_of(7)
                for n in range(2):
                    bank, free = g_full_at(0, l, ("pool", n))
                    for t in range(2):
                        c = 2 * n + t
                        ins = act.activation(ybr[:, 4 + c, :], two(bank)[:, t, :], ACT.Copy,
                                             scale=lv[:, L_PS + c:L_PS + c + 1])
                    ins.then_inc(free, 1)
                for i in range(ATT_STEPS):
                    if i < 2 * HEADS:
                        used = at(l, NM, m_of[0][("pt", i - 2)] + 1) if i >= 2 else None
                        exps((at(l, 2 * HEADS, i), i % 2), logit, prob, used)
                    for what in STEP_UNITS.get(i, ()):
                        if what[0] == "gates":
                            bank, free = g_full_at(0, l, what)
                            n = what[1]
                            act.activation(gates[:, 2 * n:2 * n + 2, :], two(bank), ACT.Exp, scale=-1.0)\
                                .then_inc(free, 1)
                    if 0 <= i - 1 < 2 * HEADS:
                        copy_turned(0, l, i - 1, (), probT)
                    if 0 <= i - 2 < 2 * HEADS:
                        s = i - 2
                        bank, free = m_full_at(0, l, ("pv", s))
                        rows = slice(DH * (s % 2), DH * (s % 2) + DH)
                        y_tile = 8 * (s // HEADS) + (s % HEADS) // 2
                        act.activation(ybr[rows, y_tile, :], bank[rows, 0:S], ACT.Copy).then_inc(free, 1)
                root(0, l, ("norm", 2))
                add_shift(l, 2, 6)
                silus(0, l, ("gate", 1, 0))

            L2 = LAYERS1
            for layer in range(LAYERS2):
                root(1, L2, (layer, "norm", 0))
                if layer % 3 == 0:
                    for p in range(4):
                        bank, free = g_full_at(1, L2, (layer, "conv", p))
                        act.activation(cv_c[:, 2 * p:2 * p + 2, :], two(bank), ACT.Copy).then_inc(free, 1)
                elif layer == 1:
                    act.wait_ge(lam_abs, 1)
                    act.activation(lamb[:, 3, :], lamb[:, 2, :], ACT.Exp, scale=-1.0).then_inc(lam_exp, 1)
                    for p in range(5):
                        bank, free = g_full_at(1, L2, (1, "rec", p))
                        act.activation(r_raw[:, 2 * p:2 * p + 2, :], two(bank), ACT.Copy).then_inc(free, 1)
                    for t in range(LT):
                        bank, free = g_full_at(1, L2, (1, "ri", t))
                        act.activation(r_r[:, t, :], bank[:, 0:S], ACT.Sigmoid, bias=v2[:, V_LAB + t:V_LAB + t + 1])\
                            .then_inc(sig_ready, 1)
                        act.activation(r_i[:, t, :], bank[:, S:2 * S], ACT.Sigmoid,
                                       bias=v2[:, V_LXB + t:V_LXB + t + 1]).then_inc(free, 1)
                    act.wait_ge(lam_ready, 1)
                    act.wait_ge(sig_ready, LT)
                    for t in range(LT):
                        act.activation(r_a[:, t, :], r_r[:, t, :], ACT.Exp, scale=lam8[:, t:t + 1])
                        act.activation(r_t[:, t, :], r_r[:, t, :], ACT.Tanh, scale=lam8[:, LT + t:LT + t + 1])\
                            .then_inc(decay_exp, 1)
                    for n in range(2):
                        act.wait_ge(var_ready, n + 1)
                        act.activation(r_t[:, 5 * n:5 * n + 5, :], r_t[:, 5 * n:5 * n + 5, :], ACT.Sqrt)\
                            .then_inc(var_root, 1)
                    for p in range(5):
                        bank, free = g_full_at(1, L2, (1, "gelu", p))
                        act.activation(r_g[:, 2 * p:2 * p + 2, :], two(bank), ACT.Gelu_apprx_tanh).then_inc(free, 1)
                else:
                    for n in range(2):
                        act.wait_ge(angle_ready, n + 1)
                        act.activation((cosT, sinT)[n][0:ROPE, :], (cosT, sinT)[n][0:ROPE, :], ACT.Sin)\
                            .then_inc(sincos_ready, 1)
                    for n in range(3):
                        bank, free = g_full_at(1, L2, (2, "cdown", n))
                        if n < 2:
                            act.activation(c_lat[:, 2 * n:2 * n + 2, :], two(bank), ACT.Copy)
                            act.activation(c_sq[:, 2 * n:2 * n + 2, :], two(bank), ACT.Square).then_inc(free, 1)
                        else:
                            act.activation(c_lat[:, 4, :], bank[:, 0:S], ACT.Copy)
                            act.activation(c_lat[0:ROPE, 5, :], bank[0:ROPE, S:2 * S], ACT.Copy)
                            act.activation(c_sq[:, 4, :], bank[:, 0:S], ACT.Square)
                            act.activation(c_sq[0:ROPE, 5, :], bank[0:ROPE, S:2 * S], ACT.Square).then_inc(free, 1)
                    for i, (name, n, rows) in enumerate((("cq", QL, P), ("ckv", KVL, P), ("kr", ROPE, ROPE))):
                        bank, free = m_full_at(1, L2, (2, name))
                        act.activation(lroot[0:rows, i, :], bank[0:rows, 0:S], ACT.Sqrt, bias=eps[0:rows, :],
                                       scale=1.0 / n).then_inc(free, 1)

                    def q_root(hd):
                        bank, free = m_full_at(1, L2, (2, "qn", hd))
                        act.activation(hsq[:, hd % 2, 0:S], bank[:, 0:S], ACT.Sqrt, bias=eps, scale=1.0 / NOPE)
                        act.activation(hsq[0:ROPE, hd % 2, S:2 * S], bank[0:ROPE, S:2 * S], ACT.Sqrt,
                                       bias=eps[0:ROPE, :], scale=1.0 / ROPE).then_inc(free, 1)

                    for hd in range(HEADS):
                        bank, free = g_full_at(1, L2, (2, "q", hd))
                        if hd >= 2:
                            act.wait_ge(head_ready, hd - 1)
                        act.activation(qn[:, hd, :], bank[:, 0:S], ACT.Copy)
                        act.activation(qr[0:ROPE, hd, :], bank[0:ROPE, S:2 * S], ACT.Copy)
                        act.activation(hsq[:, hd % 2, 0:S], bank[:, 0:S], ACT.Square)
                        act.activation(hsq[0:ROPE, hd % 2, S:2 * S], bank[0:ROPE, S:2 * S], ACT.Square)\
                            .then_inc(free, 1)
                        if hd >= 1:
                            q_root(hd - 1)
                    for n in range(4):
                        bank, free = g_full_at(1, L2, (2, "v", n))
                        act.activation(mla_v[:, n % 2, 4 * VD * (n // 2):4 * VD * (n // 2 + 1)], bank[:, :], ACT.Copy)\
                            .then_inc(free, 1)
                    q_root(HEADS - 1)
                    for hd in range(HEADS + 1):
                        if hd < HEADS:
                            bank, free = g_full_at(1, L2, (2, "k", hd))
                            act.wait_ge(head_ready, HEADS + hd - 1)
                            act.activation(kn[:, hd, :], bank[:, 0:S], ACT.Copy)
                            act.activation(hsq[:, hd % 2, 0:S], bank[:, 0:S], ACT.Square).then_inc(free, 1)
                        if hd >= 1:
                            bank, free = m_full_at(1, L2, (2, "kn", hd - 1))
                            act.activation(hsq[:, (hd - 1) % 2, 0:S], bank[:, 0:S], ACT.Sqrt, bias=eps,
                                           scale=1.0 / NOPE).then_inc(free, 1)
                    for i in range(HEADS + 2):
                        if i < HEADS:
                            used = at(L2, NM, m_of[1][(2, "pt", i - 2)] + 1) if i >= 2 else None
                            exps((2 * HEADS * LAYERS1 + i, i % 2), m_logit, m_prob, used)
                        if 0 <= i - 1 < HEADS:
                            copy_turned(1, L2, i - 1, (2,), m_probT)
                        if 0 <= i - 2 < HEADS:
                            bank, free = m_full_at(1, L2, (2, "pv", i - 2))
                            act.activation(mla_y[:, i - 2, :], bank[:, 0:S], ACT.Copy).then_inc(free, 1)
                root(1, L2, (layer, "norm", 1))
                silus(1, L2, (layer, "gate", 0))

        @block.vector
        def _(dve):
            done = [0]
            for n, free in enumerate(g_free + m_free + [g_full]):
                dve.memset(opened[:, n:n + 1], 0.0).then_inc(free, 1)
            base = [0]

            def step(ins):
                done[0] += 1
                ins.then_inc(dve_step, 1)

            def settle(l):
                dve.wait_ge(dve_step, base[0] + at(l, DVE_PER, done[0]))

            def g_full_at(b, l, name):
                t = g_of[b][name]
                dve.wait_ge(g_full, at(l, NG, t + 1) + 1)
                return gbank(t), g_free[t % BANKS]

            def m_full_at(b, l, name):
                t = m_of[b][name]
                dve.wait_ge(m_full, at(l, NM, t + 1))
                return mbank(t), m_free[t % BANKS]

            def squares(l, p, stage):
                xp = x[:, 2 * p:2 * p + 2, :]
                if p == 0:
                    dve.tensor_tensor(tiled(sqacc[:, :], 2), xp, xp, ALU.mult).then_inc(x_ready, 1)
                    return
                dve.wait_ge(x_ready, stage * 4 + p)
                step(dve.tensor_tensor(tiled(sqx[:, :], 2), xp, xp, ALU.mult))
                settle(l)
                dve.tensor_tensor(sqacc[:, :], sqacc[:, :], sqx[:, :], ALU.add).then_inc(x_ready, 1)

            def residual(b, l, names, gate, stage, last=False):
                for p, name in enumerate(names):
                    bank, free = g_full_at(b, l, name)
                    if gate is None:
                        dve.tensor_tensor(x[:, 2 * p:2 * p + 2, :], two(bank), x[:, 2 * p:2 * p + 2, :], ALU.add)\
                            .then_inc(free, 1)
                    else:
                        for t in range(2):
                            k = 2 * p + t
                            ins = dve.scalar_tensor_tensor(out=x[:, k, :], in0=two(bank)[:, t, :],
                                                           scalar=gate[:, k:k + 1], in1=x[:, k, :],
                                                           op0=ALU.mult, op1=ALU.add)
                            if t:
                                ins.then_inc(free, 1)
                            else:
                                step(ins)
                    if not last:
                        g_taken(dve, b, l, name)
                        settle(l)
                        squares(l, p, stage)

            def norm(b, l, name, gain, out_sem):
                m_taken(dve, b, l, name)
                step(dve.reciprocal(rs[:, S:2 * S], rs[:, 0:S]))
                settle(l)
                for k in range(KT):
                    dve.scalar_tensor_tensor(out=h[:, k, :], in0=x[:, k, :], scalar=gain[:, k:k + 1],
                                             in1=rs[:, S:2 * S], op0=ALU.mult, op1=ALU.mult).then_inc(out_sem, 1)

            def gate_up(b, l, gate0):
                g0 = g_of[b][gate0]
                dve.wait_ge(g_full, at(l, NG, g0 + 2) + 1)
                dve.wait_ge(g_free[g0 % BANKS], at(l, NG // BANKS, g0 // BANKS + 1) + 1)
                dve.tensor_tensor(act_f[:, 0:2 * S], gbank(g0 + 1)[:, :], silu_g[:, 0, :], ALU.mult)\
                    .then_inc(g_free[(g0 + 1) % BANKS], 1)
                with dve.Fori(0, (FJ - 1) // 2) as i:
                    for s in range(2):
                        g = g0 + 2 + 2 * s
                        dve.wait_ge(g_full, at(l, NG, g + 2) + 4 * i + 1)
                        dve.wait_ge(g_free[g % BANKS], at(l, NG // BANKS, g // BANKS + 1) + i + 1)
                        dve.tensor_tensor(act_f[:, bass.ds(4 * S * i + 2 * S * (1 + s), 2 * S)],
                                          gbank(g + 1)[:, :], silu_g[:, (1 + s) % 2, :], ALU.mult)\
                            .then_inc(g_free[(g + 1) % BANKS], 1)

            def mod_rows(l, row, n):
                bank, free = m_full_at(0, l, ("mod", row))
                c = slice(KT * row, KT * (row + n))
                dve.tensor_tensor(mod[:, c], bank[:, 0:KT * n], lv[:, L_BADA + KT * row:L_BADA + KT * (row + n)],
                                  ALU.add).then_inc(free, 1)
                m_taken(dve, 0, l, ("mod", row))

            def gain_of(l, n, row):
                c = slice(KT * n, KT * (n + 1))
                step(dve.scalar_tensor_tensor(out=gains[:, c], in0=mod[:, KT * row:KT * (row + 1)], scalar=1.0,
                                              in1=lv[:, L_GAIN + KT * n:L_GAIN + KT * (n + 1)],
                                              op0=ALU.add, op1=ALU.mult))
                settle(l)
                return gains[:, c]

            def halve(l, row):
                c = slice(KT * row, KT * (row + 1))
                step(dve.tensor_scalar(mod[:, c], mod[:, c], 0.5, None, ALU.mult))
                settle(l)

            def magnitude(z, az, ready):
                dve.scalar_tensor_tensor(out=az, in0=z, scalar=-1.0, in1=z, op0=ALU.mult, op1=ALU.max)\
                    .then_inc(ready, 1)

            def softplus_neg(l, z, e, q, q2, p, t):
                def then(ins):
                    step(ins)
                    settle(l)

                then(dve.tensor_scalar(q, e, 2.0, None, ALU.add))
                then(dve.reciprocal(q2, q))
                then(dve.tensor_tensor(q, e, q2, ALU.mult))
                then(dve.tensor_tensor(q2, q, q, ALU.mult))
                then(dve.tensor_scalar(p, q2, 1.0 / 17, None, ALU.mult))
                for k in range(7, 0, -1):
                    then(dve.scalar_tensor_tensor(out=p, in0=p, scalar=1.0 / (2 * k + 1), in1=q2,
                                                  op0=ALU.add, op1=ALU.mult))
                then(dve.scalar_tensor_tensor(out=p, in0=p, scalar=1.0, in1=q, op0=ALU.add, op1=ALU.mult))
                then(dve.tensor_scalar(q, z, -1.0, 0.0, ALU.mult, ALU.max))
                return dve.scalar_tensor_tensor(out=t, in0=p, scalar=2.0, in1=q, op0=ALU.mult, op1=ALU.add)

            def soft_max(b, l, name, n, s, lg, bias0, bias1, slot_read):
                bank, free = m_full_at(b, l, name)
                if slot_read:
                    dve.wait_ge(exp_ready, n - 1)
                dve.memset(small[:, 12:13], 0.0)
                c = 6 * s
                step(dve.tensor_tensor_reduce(out=lg[:, s, 0:P], in0=bank[:, 0:P], in1=bias0, scale=1.0,
                                              scalar=-3e38, op0=ALU.add, op1=ALU.max,
                                              accum_out=small[:, 14 + c // 3:15 + c // 3]))
                dve.tensor_tensor_reduce(out=lg[:, s, P:3 * P], in0=bank[:, P:3 * P], in1=bias1, scale=1.0,
                                         scalar=-3e38, op0=ALU.add, op1=ALU.max,
                                         accum_out=small[:, 15 + c // 3:16 + c // 3]).then_inc(free, 1)
                m_taken(dve, b, l, name)
                settle(l)
                dve.tensor_scalar(small[:, c:c + 2], small[:, 14 + c // 3:16 + c // 3], -1.0, None, ALU.mult)\
                    .then_inc(max_ready, 1)

            def soft_norm(l, n, s, pr):
                c = 6 * s
                dve.wait_ge(exp_ready, n + 1)
                step(dve.reciprocal(small[:, c + 4:c + 6], small[:, c + 2:c + 4]))
                settle(l)
                step(dve.tensor_scalar(pr[:, s, 0:P], pr[:, s, 0:P], small[:, c + 4:c + 5], None, ALU.mult))
                dve.tensor_scalar(pr[:, s, P:3 * P], pr[:, s, P:3 * P], small[:, c + 5:c + 6], None, ALU.mult)\
                    .then_inc(prob_ready, 1)

            def merge(l, what):
                _, n, u = what
                for i in range(2):
                    bank, free = g_full_at(0, l, what + (i,))
                    pp = 2 * u + i
                    gate = gates[:, 8 * n + 2 * pp:8 * n + 2 * pp + 2, :]
                    settle(l)
                    if n == 1:
                        dve.tensor_tensor(h[:, 2 * pp:2 * pp + 2, :], two(bank), gate, ALU.mult).then_inc(free, 1)
                        continue
                    if n == 2 and (u or i):
                        dve.wait_ge(merged_ready, at(l, 4, pp))
                    dve.tensor_tensor(tiled(sqx[:, :], 2), two(bank), gate, ALU.mult).then_inc(free, 1)
                    g_taken(dve, 0, l, what + (i,))
                    if n == 0:
                        g_taken(dve, 0, l, ("branch", 1, u, i))
                    ins = dve.tensor_tensor(h[:, 2 * pp:2 * pp + 2, :], h[:, 2 * pp:2 * pp + 2, :],
                                            tiled(sqx[:, :], 2), ALU.add)
                    if n == 2:
                        ins.then_inc(merged_ready, 1)
                    else:
                        step(ins)

            dve.wait_ge(rel_loaded, 16)
            dve.tensor_copy(arena[0:LAYERS1 * HEADS, REL - 1:EXT],
                            arena[0:LAYERS1 * HEADS, REL - 2:REL - 1].to_broadcast([LAYERS1 * HEADS, EXT - REL + 1]))\
                .then_inc(rel_padded, 1)
            dve.wait_ge(x_loaded, 16)
            for p in range(4):
                squares(0, p, 0)
            base[0], done[0] = done[0], 0
            dve.wait_ge(const_loaded, 32)

            with dve.Fori(0, LAYERS1) as l:
                dve.wait_ge(lv_loaded, at(l, 16, 16))
                mod_rows(l, 0, 2)
                norm(0, l, ("norm", 0), gain_of(l, 0, 1), h_scaled)
                gate_up(0, l, ("gate", 0, 0))
                mod_rows(l, 2, 1)
                halve(l, 2)
                residual(0, l, [("down", 0, p) for p in range(4)], mod[:, 2 * KT:3 * KT], l * 3 + 1)

                mod_rows(l, 3, 1)
                mod_rows(l, 4, 1)
                step(dve.tensor_scalar(qgain[:, 0:4:2], lv[:, L_QK:L_QK + 4:2], DH ** -0.5, None, ALU.mult))
                step(dve.tensor_copy(qgain[:, 1:4:2], lv[:, L_QK + 1:L_QK + 4:2]))
                norm(0, l, ("norm", 1), gain_of(l, 1, 4), h_scaled)

                bank, free = m_full_at(0, l, "f")
                z, az, e, q, q2, pl, sp_z = (fz[0:HEADS, n, :] for n in range(1, 8))
                dve.tensor_scalar(z, bank[0:HEADS, 0:S], lv[0:HEADS, L_FB:L_FB + 1], None, ALU.add).then_inc(free, 1)
                m_taken(dve, 0, l, "f")
                magnitude(z, az, f_abs)

                g_taken(dve, 0, l, ("u", 1))
                src = tiled(u_in, 4)
                bufs = [tiled(win[:, n, :], 4) for n in range(2)]
                for n in range(4):
                    sh, dst = 1 << n, bufs[n % 2]
                    step(dve.tensor_copy(dst[:, n:4, 0:sh], src[:, n:4, 0:sh]))
                    step(dve.tensor_tensor(dst[:, n:4, sh:S], src[:, n:4, sh:S], src[:, n:4, 0:S - sh], ALU.add))
                    settle(l)
                    src = dst
                for n in range(2):
                    step(dve.tensor_tensor(bufs[1][:, n:4:2, :], bufs[n][:, n:4:2, :], inv_count[:, n:4:2, :],
                                           ALU.mult))
                settle(l)
                dve.tensor_tensor(win[:, 1, :], win[:, 1, :], u_in, ALU.subtract).then_inc(diff_ready, 1)

                dve.wait_ge(f_exp, at(l, 1, 1))
                step(softplus_neg(l, z, e, q, q2, pl, sp_z))
                settle(l)
                dve.tensor_tensor_scan(out=fz[0:HEADS, 0, :], data0=ones_row[0:HEADS, :], data1=sp_z, initial=0.0,
                                       op0=ALU.mult, op1=ALU.add).then_inc(decay_ready, 1)

                for n in range(8):
                    m_taken(dve, 0, l, ("qk", n))
                    step(dve.reciprocal(sqb[:, n % 2, :], sqb[:, n % 2, :]))
                    settle(l)
                    dve.scalar_tensor_tensor(out=qk[:, 2 * n:2 * n + 2, :], in0=qk[:, 2 * n:2 * n + 2, :],
                                             scalar=qgain[:, n // 2:n // 2 + 1], in1=tiled(sqb[:, n % 2, :], 2),
                                             op0=ALU.mult, op1=ALU.mult).then_inc(qk_ready, 1)
                dve.wait_ge(relb_loaded, at(l, 16, 16))
                step(dve.memset(relb[0:CHUNK, :, 0:CHUNK], NEG))
                settle(l)

                for i in range(ATT_STEPS):
                    if i < 2 * HEADS:
                        a, hd = i // HEADS, i % HEADS
                        n = at(l, 2 * HEADS, i)
                        if a:
                            b0, b1 = causal[:, P:S], causal
                        else:
                            b0, b1 = relb[:, hd, 0:P][:, ::-1], relb[:, hd, :][:, ::-1]
                        soft_max(0, l, ("s", i), n, i % 2, logit, b0, b1, i >= 2)
                        soft_norm(l, n, i % 2, prob)
                    for what in STEP_UNITS.get(i, ()):
                        if what[0] == "gates":
                            g_taken(dve, 0, l, what)
                            gt = gates[:, 2 * what[1]:2 * what[1] + 2, :]
                            step(dve.tensor_scalar(gt, gt, 1.0, None, ALU.add))
                            settle(l)
                            step(dve.reciprocal(gt, gt))
                        else:
                            merge(l, what)
                for u in range(2):
                    merge(l, ("branch", 2, u))
                mod_rows(l, 5, 1)
                residual(0, l, [("wout", p) for p in range(4)], mod[:, 5 * KT:6 * KT], l * 3 + 2)

                mod_rows(l, 6, 1)
                mod_rows(l, 7, 1)
                norm(0, l, ("norm", 2), gain_of(l, 2, 7), h_scaled)
                gate_up(0, l, ("gate", 1, 0))
                mod_rows(l, 8, 1)
                halve(l, 8)
                residual(0, l, [("down", 1, p) for p in range(4)], mod[:, 8 * KT:9 * KT], l * 3 + 3)
                assert done[0] == DVE_PER, done

            done[0] = 0
            L2 = LAYERS1

            def then(ins):
                step(ins)
                settle(L2)

            def causal_conv(src, dst, taps, bias, ready=None):
                if bias is None:
                    then(dve.tensor_scalar(dst, src, taps[0], None, ALU.mult))
                else:
                    then(dve.tensor_scalar(dst, src, taps[0], bias, ALU.mult, ALU.add))
                for lag in range(1, len(taps)):
                    ins = dve.scalar_tensor_tensor(out=dst[:, lag:S], in0=src[:, 0:S - lag], scalar=taps[lag],
                                                   in1=dst[:, lag:S], op0=ALU.mult, op1=ALU.add)
                    if ready is not None and lag == len(taps) - 1:
                        ins.then_inc(ready, 1)
                    else:
                        then(ins)

            def conv_mixer(layer):
                j = layer // 3
                for p in range(4):
                    g_taken(dve, 1, L2, (layer, "conv", p))
                    bank, free = g_full_at(1, L2, (layer, "conv", 4 + p))
                    pair = slice(2 * p, 2 * p + 2)
                    dve.tensor_tensor(cv_c[:, pair, :], two(bank), cv_c[:, pair, :], ALU.mult).then_inc(free, 1)
                    g_taken(dve, 1, L2, (layer, "conv", 4 + p))
                    for k in (2 * p, 2 * p + 1):
                        tap = [V_CONV + (3 * j + 2 - lag) * KT + k for lag in range(3)]
                        causal_conv(cv_c[:, k, :], cv_o[:, k, :], [v2[:, c:c + 1] for c in tap], None)
                for p in range(4):
                    bank, free = g_full_at(1, L2, (layer, "conv", 8 + p))
                    pair = slice(2 * p, 2 * p + 2)
                    dve.tensor_tensor(mix_y[:, pair, :], two(bank), cv_o[:, pair, :], ALU.mult).then_inc(free, 1)

            def lru_mixer():
                dve.wait_ge(lam_exp, 1)
                lam = v2[:, V_LAM:V_LAM + LT]
                then(softplus_neg(L2, lam, *(lamb[:, n, :] for n in range(3, 8))))
                then(dve.tensor_scalar(lam8[:, 0:LT], lamb[:, 7, :], -8.0, None, ALU.mult))
                dve.tensor_scalar(lam8[:, LT:2 * LT], lamb[:, 7, :], 8.0, None, ALU.mult).then_inc(lam_ready, 1)
                for p in range(5):
                    g_taken(dve, 1, L2, (1, "rec", p))
                    for k in (2 * p, 2 * p + 1):
                        tap = [V_LCONV + (3 - lag) * LT + k for lag in range(4)]
                        causal_conv(r_raw[:, k, :], r_rec[:, k, :], [v2[:, c:c + 1] for c in tap],
                                    v2[:, V_LCB + k:V_LCB + k + 1], mix_ready)
                g_taken(dve, 1, L2, (1, "ri", LT - 2))
                g_taken(dve, 1, L2, (1, "ri", LT - 1))
                dve.wait_ge(mix_ready, LT)
                step(dve.tensor_tensor(r_i, r_i, r_rec, ALU.mult))
                settle(L2)
                for n in range(2):
                    s = slice(5 * n, 5 * n + 5)
                    dve.wait_ge(decay_exp, 5 * (n + 1))
                    then(dve.tensor_tensor(r_raw[:, s, :], r_a[:, s, :], r_a[:, s, :], ALU.mult))
                    dve.scalar_tensor_tensor(out=r_t[:, s, :], in0=r_raw[:, s, :], scalar=1.0, in1=r_t[:, s, :],
                                             op0=ALU.add, op1=ALU.mult).then_inc(var_ready, 1)
                for n in range(2):
                    s = slice(5 * n, 5 * n + 5)
                    dve.wait_ge(var_root, n + 1)
                    dve.wait_ge(var_ready, 2)
                    then(dve.tensor_tensor(r_i[:, s, :], r_i[:, s, :], r_t[:, s, :], ALU.mult))
                    for k in range(5 * n, 5 * n + 5):
                        step(dve.tensor_tensor_scan(out=r_raw[:, k, :], data0=r_a[:, k, :], data1=r_i[:, k, :],
                                                    initial=0.0, op0=ALU.mult, op1=ALU.add))
                settle(L2)
                for p in range(5):
                    g_taken(dve, 1, L2, (1, "gelu", p))
                    for k in (2 * p, 2 * p + 1):
                        dve.tensor_tensor(r_g[:, k, :], r_g[:, k, :], r_raw[:, k, :], ALU.mult).then_inc(mix_ready, 1)

            def rotary_angles():
                r = slice(0, ROPE)
                dve.wait_ge(pos_loaded, 16)
                then(dve.tensor_copy(rope_a[r, :], posi[:, :]))
                then(dve.tensor_scalar(rope_a[r, :], rope_a[r, :], cst[r, C_FREQ:C_FREQ + 1], None, ALU.mult))
                for n, (dst, turn) in enumerate(((cosT, 0.25), (sinT, 0.0))):
                    then(dve.tensor_scalar(rope_b[r, :], rope_a[r, :], 1 / TWO_PI, turn, ALU.mult, ALU.add))
                    then(dve.tensor_scalar(rope_b[r, :], rope_b[r, :], ROUND, None, ALU.add))
                    then(dve.tensor_scalar(rope_b[r, :], rope_b[r, :], -ROUND, None, ALU.add))
                    src = rope_a
                    for c in TWO_PI_PARTS:
                        then(dve.scalar_tensor_tensor(out=dst[r, :], in0=rope_b[r, :], scalar=-c, in1=src[r, :],
                                                      op0=ALU.mult, op1=ALU.add))
                        src = dst
                    then(dve.tensor_scalar(dst[r, :], dst[r, :], turn * TWO_PI, PI_BELOW, ALU.add, ALU.min))
                    dve.tensor_scalar(dst[r, :], dst[r, :], -PI_BELOW, None, ALU.max).then_inc(angle_ready, 1)

            def rope(name, t, count):
                r = slice(0, ROPE)
                bank, free = m_full_at(1, L2, name)
                if count:
                    dve.wait_ge(rope_ready, count)
                dve.tensor_tensor(rope_b[r, :], bank[r, 0:S], sinT[r, :], ALU.mult).then_inc(free, 1)
                step(dve.tensor_tensor(rope_c[r, :], t, cosT[r, :], ALU.mult))
                m_taken(dve, 1, L2, name)
                settle(L2)
                dve.tensor_tensor(t, rope_b[r, :], rope_c[r, :], ALU.add).then_inc(rope_ready, 1)

            def mla_mixer():
                scale = (NOPE + ROPE) ** -0.5
                then(dve.tensor_scalar(qgain[:, 0:1], v2[:, V_QNN:V_QNN + 1], scale, None, ALU.mult))
                then(dve.tensor_scalar(qgain[:, 1:2], v2[:, V_QRN:V_QRN + 1], scale, None, ALU.mult))
                rotary_angles()
                for i, (name, tiles_, rows, col) in enumerate((("cq", (0, 1, 2), P, V_QN), ("ckv", (3, 4), P, V_KVN),
                                                              ("kr", (5,), ROPE, V_KRN))):
                    m_taken(dve, 1, L2, (2, name))
                    then(dve.reciprocal(lroot[0:rows, i, :], lroot[0:rows, i, :]))
                    for n, k in enumerate(tiles_):
                        ins = dve.scalar_tensor_tensor(out=c_lat[0:rows, k, :], in0=c_lat[0:rows, k, :],
                                                       scalar=v2[0:rows, col + n:col + n + 1],
                                                       in1=lroot[0:rows, i, :], op0=ALU.mult, op1=ALU.mult)
                        if k == tiles_[-1]:
                            ins.then_inc(lat_ready, 1)
                        else:
                            step(ins)
                dve.wait_ge(sincos_ready, 2)
                dve.wait_ge(lat_ready, 3)
                rope((2, "krot"), c_lat[0:ROPE, 5, :], 0)
                for hd in range(HEADS + 1):
                    if hd < HEADS:
                        m_taken(dve, 1, L2, (2, "qn", hd))
                        s = hd % 2
                        step(dve.reciprocal(hsq[:, s, 0:S], hsq[:, s, 0:S]))
                        step(dve.reciprocal(hsq[0:ROPE, s, S:2 * S], hsq[0:ROPE, s, S:2 * S]))
                        settle(L2)
                        step(dve.scalar_tensor_tensor(out=qn[:, hd, :], in0=qn[:, hd, :], scalar=qgain[:, 0:1],
                                                      in1=hsq[:, s, 0:S], op0=ALU.mult, op1=ALU.mult))
                        dve.scalar_tensor_tensor(out=qr[0:ROPE, hd, :], in0=qr[0:ROPE, hd, :],
                                                 scalar=qgain[0:ROPE, 1:2], in1=hsq[0:ROPE, s, S:2 * S],
                                                 op0=ALU.mult, op1=ALU.mult).then_inc(head_ready, 1)
                    if hd >= 1:
                        rope((2, "qrot", hd - 1), qr[0:ROPE, hd - 1, :], hd)
                for hd in range(HEADS):
                    m_taken(dve, 1, L2, (2, "kn", hd))
                    s = hd % 2
                    then(dve.reciprocal(hsq[:, s, 0:S], hsq[:, s, 0:S]))
                    dve.scalar_tensor_tensor(out=kn[:, hd, :], in0=kn[:, hd, :], scalar=v2[:, V_KNN:V_KNN + 1],
                                             in1=hsq[:, s, 0:S], op0=ALU.mult, op1=ALU.mult).then_inc(head_ready, 1)
                for i in range(HEADS):
                    n = 2 * HEADS * LAYERS1 + i
                    soft_max(1, L2, (2, "s", i), n, i % 2, m_logit, causal[:, P:S], causal, i >= 2)
                    soft_norm(L2, n, i % 2, m_prob)

            magnitude(v2[:, V_LAM:V_LAM + LT], lamb[:, 2, :], lam_abs)
            for layer in range(LAYERS2):
                stage = 3 * LAYERS1 + 2 * layer
                norm(1, L2, (layer, "norm", 0), v2[:, V_MIX + KT * layer:V_MIX + KT * (layer + 1)], h_ready)
                if layer % 3 == 0:
                    conv_mixer(layer)
                elif layer == 1:
                    lru_mixer()
                else:
                    mla_mixer()
                residual(1, L2, [(layer, "out", p) for p in range(4)], None, stage + 1)
                norm(1, L2, (layer, "norm", 1), v2[:, V_FFN + KT * layer:V_FFN + KT * (layer + 1)], h_ready)
                gate_up(1, L2, (layer, "gate", 0))
                residual(1, L2, [(layer, "down", p) for p in range(4)], None, stage + 2, layer == LAYERS2 - 1)


_STREAMED = ["w_ada", "ffn_w_gate", "ffn_w_up", "ffn_w_down", "w_in", "rel_bias", "w_branch", "w_out",
             "positions_2", "conv_w_in_2", "conv_w_out_2", "lru_w_in_2", "lru_gate_a_w_2", "lru_gate_x_w_2",
             "lru_w_out_2", "mla_w_down_2", "mla_w_uq_2", "mla_w_ukv_2", "mla_w_o_2", "ffn_w_gu_2",
             "ffn_w_down_2"]


def constants():
    c = np.zeros((P, C_ALL), np.float32)
    p = np.arange(P)
    c[:, C_IDENT:C_IDENT + P] = np.eye(P)
    c[:, C_HALVES:C_HALVES + P] = p[:, None] // DH == p[None, :] // DH
    c[:, C_ONES:C_ONES + S] = 1
    c[:, C_CAUSAL:C_CAUSAL + S] = np.where(np.arange(S)[None, :] - P > p[:, None], NEG, 0)
    for g, width in enumerate(WINDOWS):
        c[:, C_INV + S * g:C_INV + S * (g + 1)] = 1 / np.minimum(np.arange(S) + 1, width)
    for hd in range(HEADS):
        c[hd, C_SEL + P * hd:C_SEL + P * (hd + 1)] = 1
    half = ROPE // 2
    for n in range(half):
        c[n + half, C_ROT + n] = -1
        c[n, C_ROT + n + half] = 1
    c[:, C_FREQ] = 10000.0 ** (-2.0 * (p % half) / ROPE)
    c[:, C_EPS] = EPS
    return c


def columns(a):
    return a.reshape(-1, P).T


def padded(a):
    return np.pad(a.reshape(-1, 1), ((0, P - a.size), (0, 0)))


def kernel(**inputs):
    import concourse.bacc as bacc
    from concourse.bass_utils import run_bass_kernel_spmd

    a = {name: np.asarray(value) for name, value in inputs.items()}
    arrays = {name: np.ascontiguousarray(a[name]) for name in _STREAMED}
    arrays["x"] = np.ascontiguousarray(a["x"][0].reshape(S, KT, P).transpose(2, 1, 0))
    arrays["c"] = np.ascontiguousarray(columns(a["c"]))
    arrays["constants"] = constants()
    arrays["vectors_1"] = np.stack([np.concatenate([
        columns(a["b_ada"][l]), columns(a["norm_gain"][l]), np.tile(a["qk_gain"][l], (1, 2)).T,
        padded(a["forget_bias"][l]), columns(a["pool_scale"][l]),
        a["w_in"][l][:, 7 * MIX_COLS:G_COL].reshape(KT, P, HEADS).transpose(1, 0, 2).reshape(P, KT * HEADS),
        a["w_pool"][l].transpose(1, 0, 2).reshape(P, 4 * P)], axis=1) for l in range(LAYERS1)])
    arrays["vectors_2"] = np.concatenate([
        columns(a["mix_norm_2"]), columns(a["ffn_norm_2"]), columns(a["conv_w_2"]), columns(a["lru_conv_w_2"]),
        columns(a["lru_conv_b_2"]), columns(a["lru_gate_a_b_2"]), columns(a["lru_gate_x_b_2"]),
        columns(a["lru_lambda_2"]), columns(a["mla_q_norm_2"]), columns(a["mla_kv_norm_2"]),
        columns(a["mla_qn_norm_2"]), padded(a["mla_qr_norm_2"]), columns(a["mla_kn_norm_2"]),
        padded(a["mla_kr_norm_2"])], axis=1)

    nc = bacc.Bacc("TRN2", target_bir_lowering=False, num_devices=1)
    w = {}
    for name, array in arrays.items():
        w[name] = nc.dram_tensor("in_" + name, array.shape, mybir.dt.from_np(array.dtype), kind="ExternalInput").ap()
    out = nc.dram_tensor("out", (P, KT, S), F32, kind="ExternalOutput").ap()
    build_program(nc, w, out)
    r = run_bass_kernel_spmd(nc, [{"in_" + name: array for name, array in arrays.items()}], core_ids=[0])
    return r.results[0]["out"].transpose(2, 1, 0).reshape(1, S, D)
```

```python
from contextlib import ExitStack

import concourse.bass as bass
import numpy as np
from concourse import mybir

F32 = mybir.dt.float32
F32R = mybir.dt.float32r
I32 = mybir.dt.int32
ALU = mybir.AluOpType
ACT = mybir.ActivationFunctionType
AX_X = mybir.AxisListType.X

P = 128
S = 256
D = 1024
KT = D // P
F = 2816
FT = F // P
UC = 256
FJ = F // UC
THIRDS = ((0, 8), (8, 16), (16, FT))
FFN_UNITS = 2 * FJ + 4 * len(THIRDS)
GU = 2 * FJ
SLOTS = 4
BANKS = 4
LAYERS1 = 2
LAYERS2 = 4
HEADS = 8
DH = 64
CHUNK = 64
N_MOD = 9
EPS = 1e-6
NEG = -1e30
MIX_COLS = 512
G_COL = 7 * MIX_COLS + HEADS
WINDOWS = (2, 4, 8, 16)
REL = 257
EXT = 384
LRU_W = 1280
LT = LRU_W // P
SLOT_COLS = LT * UC
QL, KVL, ROPE, NOPE, VD = 384, 256, 64, 128, 128
MLA_DOWN = QL + KVL + ROPE
CQ, CKV = QL // P, KVL // P
TWO_PI = 6.283185307179586
TWO_PI_PARTS = (6.28125, 1.93500518798828125e-3, 3.0199099819e-7)
PI_BELOW = 3.1415925
ROUND = 1.5 * 2 ** 23
ARENA = 24320
DVE_PER = 138

C_ONES, C_EPS, C_IDENT, C_HALVES, C_CAUSAL, C_INV, C_SEL, C_ROT, C_FREQ, C_ALL = np.cumsum(
    [0, S, 1, P, P, S, 4 * S, HEADS * P, ROPE, 1]).tolist()

L_BADA, L_GAIN, L_QK, L_FB, L_PS, L_WF, L_WP = np.cumsum(
    [0, N_MOD * KT, 3 * KT, 4, 1, 4, KT * HEADS]).tolist()
L_ALL = L_WP + 4 * P

V_MIX, V_FFN, V_CONV, V_LCONV, V_LCB, V_LAB, V_LXB, V_LAM, V_QN, V_KVN, V_QNN, V_QRN, V_KNN, V_KRN = np.cumsum(
    [0, 4 * KT, 4 * KT, 2 * 3 * KT, 4 * LT, LT, LT, LT, LT, CQ, CKV, 1, 1, 1]).tolist()
V_ALL = V_KRN + 1


def plan_block1():
    units, g, m = [], [], []

    def ffn(n):
        for j in range(FJ):
            units.extend([("gate", n, j), ("up", n, j)])
            g.extend([("gate", n, j), ("up", n, j)])
        m.append(("mod", 2 if n == 0 else 8))
        for p in range(4):
            units.extend([("down", n, p, third) for third in range(len(THIRDS))])
            g.append(("down", n, p))

    m.extend([("norm", 0), ("mod", 0)])
    ffn(0)
    m.extend([("mod", 3), ("mod", 4), ("norm", 1)])
    for u in range(2):
        units.append(("win", "u", u))
        g.append(("u", u))
    m.append("f")
    for n in range(8):
        units.append(("win", "qk", n))
        g.append(("qk", n))
        m.append(("qk", n))
    for n in range(4):
        units.append(("win", "v", n))
        g.append(("v", n))
    g.extend([("pool", 0), ("pool", 1)])
    for i in range(ATT_STEPS):
        if i < 2 * HEADS:
            m.append(("s", i))
        for what in STEP_UNITS.get(i, ()):
            units.append(what)
            g.extend([what] if what[0] == "gates" else [what + (0,), what + (1,)])
        if 0 <= i - 1 < 2 * HEADS:
            m.append(("pt", i - 1))
        if 0 <= i - 2 < 2 * HEADS:
            m.append(("pv", i - 2))
    for u in range(2):
        units.append(("branch", 2, u))
        g.extend([("branch", 2, u, 0), ("branch", 2, u, 1)])
    m.append(("mod", 5))
    for p in range(4):
        units.append(("wout", p))
        g.append(("wout", p))
    m.extend([("mod", 6), ("mod", 7), ("norm", 2)])
    ffn(1)
    return units, g, m


ATT_STEPS = 2 * HEADS + 2
STEP_UNITS = {i: [("gates", i)] for i in range(12)}
STEP_UNITS.update({12: [("branch", 1, 0)], 13: [("branch", 1, 1)], 14: [("branch", 0, 0)], 15: [("branch", 0, 1)]})


def plan_block2():
    units, g, m = [], [], []

    def plain(layer, what, n):
        for p in range(n):
            units.append((layer, what, p))
            g.append((layer, what, p))

    for layer in range(LAYERS2):
        m.append((layer, "norm", 0))
        if layer % 3 == 0:
            plain(layer, "conv", 12)
        elif layer == 1:
            plain(layer, "rec", 5)
            units.extend([(layer, "blocks", 0), (layer, "blocks", 1)])
            g.extend([(layer, "ri", t) for t in range(LT)])
            plain(layer, "gelu", 5)
        else:
            plain(layer, "cdown", 3)
            m.extend([(layer, "cq"), (layer, "ckv"), (layer, "kr"), (layer, "krot")])
            for n in range(2):
                units.append((layer, "uq", n))
                for h in range(4 * n, 4 * n + 4):
                    g.append((layer, "q", h))
                    if h >= 1:
                        m.append((layer, "qn", h - 1))
                    if h >= 2:
                        m.append((layer, "qrot", h - 2))
            units.extend([(layer, "ukv", 0), (layer, "ukv", 1)])
            g.extend([(layer, "v", n) for n in range(4)])
            m.extend([(layer, "qn", HEADS - 1), (layer, "qrot", HEADS - 2), (layer, "qrot", HEADS - 1)])
            for h in range(HEADS + 1):
                if h < HEADS:
                    g.append((layer, "k", h))
                if h >= 1:
                    m.append((layer, "kn", h - 1))
            for i in range(HEADS + 2):
                if i < HEADS:
                    m.append((layer, "s", i))
                if 0 <= i - 1 < HEADS:
                    m.append((layer, "pt", i - 1))
                if 0 <= i - 2 < HEADS:
                    m.append((layer, "pv", i - 2))
        plain(layer, "out", 4)
        m.append((layer, "norm", 1))
        for j in range(FJ):
            units.extend([(layer, "gate", j), (layer, "up", j)])
            g.extend([(layer, "gate", j), (layer, "up", j)])
        for p in range(4):
            units.extend([(layer, "down", p, third) for third in range(len(THIRDS))])
            g.append((layer, "down", p))
    return units, g, m


def build_program(nc, w, out):
    U1, G1, M1 = plan_block1()
    U2, G2, M2 = plan_block2()
    assert len(U1) % SLOTS == 0 and len(G1) % BANKS == 0 and len(M1) % BANKS == 0
    NU, NG, NM = len(U1), len(G1), len(M1)
    u_of = [{n: i for i, n in enumerate(U)} for U in (U1, U2)]
    g_of = [{n: i for i, n in enumerate(G)} for G in (G1, G2)]
    m_of = [{n: i for i, n in enumerate(M)} for M in (M1, M2)]

    split_units = [[n for n in U1 if n[0] in ("gate", "up", "down")],
                   [n for n in U2 if n[1] in ("gate", "up", "down", "conv") or (n[1] == "out" and n[0] % 3 == 0)]]
    split_of = [{n: i for i, n in enumerate(units)} for units in split_units]
    NS = len(split_units[0])

    def last_ticket():
        own = {}
        for b, U in enumerate((U1, U2)):
            for n in U:
                k = n[1:] if b else n
                pre = n[:1] if b else ()
                if n in split_of[b]:
                    continue
                if k[0] == "win":
                    t = (k[1], k[2])
                elif k[0] == "branch":
                    t = n + (1,)
                elif k[0] == "blocks":
                    t = pre + ("ri", LT - 1)
                elif k[0] == "uq":
                    t = pre + ("q", 4 * k[1] + 3)
                elif k[0] == "ukv":
                    t = pre + ("k", 4 * k[1] + 3)
                elif k[0] == "wout":
                    t = n
                else:
                    t = n
                own[b, n] = g_of[b][t]
        return own

    reader = last_ticket()

    def at(l, per, n):
        return l * per + n

    with ExitStack() as ctx:
        def sb(name, shape, dt=F32):
            return ctx.enter_context(nc.sbuf_tensor(name, shape, dt))

        def sem(name):
            return ctx.enter_context(nc.semaphore(name))

        ring = sb("ring", [P, SLOTS, SLOT_COLS])
        ada_ring = sb("ada_ring", [P, 4, D])
        ada_acc = sb("ada_acc", [P, 3, D])
        x = sb("x", [P, KT, S])
        h = sb("h", [P, KT, S])
        cst = sb("cst", [P, C_ALL])
        lv = sb("lv", [P, L_ALL])
        v2 = sb("v2", [P, V_ALL])
        cact = sb("cact", [P, KT])
        mod = sb("mod", [P, N_MOD * KT])
        gains = sb("gains", [P, 3 * KT])
        qgain = sb("qgain", [P, 4])
        sqx = sb("sqx", [P, 2 * S])
        sqacc = sb("sqacc", [P, 2 * S])
        rs = sb("rs", [P, 2 * S])
        small = sb("small", [P, 24])
        lam8 = sb("lam8", [P, 2 * LT])
        lamb = sb("lamb", [P, 8, LT])
        opened = sb("opened", [P, 2 * BANKS + 3])
        posi = sb("posi", [ROPE, S], I32)
        with ExitStack() as mixers:
            arena = mixers.enter_context(nc.sbuf_tensor("arena", [P, ARENA], F32))
        with ExitStack() as conv:
            conv.enter_context(nc.sbuf_tensor("conv_arena", [P, 3 * KT * S], F32))
            y_r = conv.enter_context(nc.sbuf_tensor("y_r", [P, 2, KT, S], F32R))
        act_r = sb("act_r", [P, 2, FT, S], F32R)
        silu_g = sb("silu_g", [P, 2, 2 * S])
        h_r = sb("h_r", [P, 2, KT, S], F32R)
        w_parts = sb("w_parts", [P, 2, 2, KT * UC], F32R)
        taken = [0]

        def part(cols):
            taken[0] += cols
            assert taken[0] <= ARENA
            return arena[:, taken[0] - cols:taken[0]]

        def tiled(ap, n):
            return ap.rearrange("p (k t) -> p k t", k=n)

        qk = tiled(part(16 * S), 16)
        vtok = part(2 * 2 * MIX_COLS).rearrange("p (a t c) -> p a t c", a=2, t=2)
        win = tiled(part(8 * S), 2)
        taken[0] -= 8 * S
        logit = tiled(part(2 * 3 * P), 2)
        prob = tiled(part(2 * 3 * P), 2)
        part(2 * S)
        u_in = part(4 * S)
        gates = tiled(part(24 * S), 24)
        relb = tiled(part(HEADS * S), HEADS)
        ybr = tiled(part(12 * S), 12)
        probT = tiled(part(2 * 3 * P), 2)
        sqb = tiled(part(2 * 2 * S), 2)
        fz = tiled(part(8 * S), 8)
        ada_wide = tiled(arena[:, 0:KT * 2 * D], KT)
        rel_pad = arena[0:LAYERS1 * HEADS, ARENA - EXT:ARENA]
        taken[0] = 0
        cv_c = tiled(part(KT * S), KT)
        cv_o = tiled(part(KT * S), KT)
        mix_y = tiled(part(KT * S), KT)
        taken[0] = 0
        r_g, r_raw, r_rec, r_r, r_i, r_a, r_t = (tiled(part(LT * S), LT) for _ in range(7))
        taken[0] = 0
        c_lat = tiled(part(6 * S), 6)
        c_sq = tiled(part(6 * S), 6)
        qn = tiled(part(HEADS * S), HEADS)
        qr = tiled(part(HEADS * S), HEADS)
        kn = tiled(part(HEADS * S), HEADS)
        mla_y = tiled(part(HEADS * S), HEADS)
        mla_v = tiled(part(2 * D), 2)
        cosT, sinT, rope_a, rope_b, rope_c = (part(S) for _ in range(5))
        hsq = tiled(part(2 * 2 * S), 2)
        lroot = tiled(part(3 * S), 3)
        m_logit, m_prob, m_probT = (tiled(part(2 * 3 * P), 2) for _ in range(3))

        ident = cst[:, C_IDENT:C_IDENT + P]
        halves = cst[:, C_HALVES:C_HALVES + P]
        ones = cst[:, C_ONES:C_ONES + P]
        ones_row = cst[:, C_ONES:C_ONES + S]
        causal = cst[:, C_CAUSAL:C_CAUSAL + S]
        inv_count = tiled(cst[:, C_INV:C_INV + 4 * S], 4)
        eps = cst[:, C_EPS:C_EPS + 1]

        psum = [ctx.enter_context(nc.psum_tensor(f"ps{b}", [P, 2 * S], F32)) for b in range(2 * BANKS)]

        def gbank(t):
            return psum[t % BANKS]

        def mbank(t):
            return psum[BANKS + t % BANKS]

        def two(bank):
            return bank[:, :].rearrange("p (t s) -> p t s", t=2)

        rel_rows = nc.dram_tensor("rel_rows", [LAYERS1 * HEADS, EXT], F32, kind="Internal")

        unit_loaded = [sem(f"unit_loaded{s}") for s in range(SLOTS)]
        g_full = sem("g_full")
        m_full = sem("m_full")
        g_free = [sem(f"g_free{b}") for b in range(BANKS)]
        m_free = [sem(f"m_free{b}") for b in range(BANKS)]
        ones_loaded = sem("ones_loaded")
        const_loaded = sem("const_loaded")
        x_loaded = sem("x_loaded")
        c_loaded = sem("c_loaded")
        rel_loaded = sem("rel_loaded")
        rel_padded = sem("rel_padded")
        rel_stored = sem("rel_stored")
        relb_loaded = sem("relb_loaded")
        relb_masked = sem("relb_masked")
        lv_loaded = sem("lv_loaded")
        pos_loaded = sem("pos_loaded")
        cact_ready = sem("cact_ready")
        ada_loaded = [sem(f"ada_loaded{s}") for s in range(4)]
        ada_step = sem("ada_step")
        ada_first = [sem(f"ada_first{s}") for s in range(KT)]
        first_rows = sem("first_rows")
        dve_step = sem("dve_step")
        x_ready = sem("x_ready")
        h_scaled = sem("h_scaled")
        h_ready = sem("h_ready")
        h_high = sem("h_high")
        w_high = sem("w_high")
        w_low = sem("w_low")
        y_high = sem("y_high")
        y_low = sem("y_low")
        act_high = sem("act_high")
        act_low = sem("act_low")
        down_part = sem("down_part")
        diff_ready = sem("diff_ready")
        qk_ready = sem("qk_ready")
        f_abs = sem("f_abs")
        f_exp = sem("f_exp")
        decay_ready = sem("decay_ready")
        max_ready = sem("max_ready")
        exp_ready = sem("exp_ready")
        prob_ready = sem("prob_ready")
        merged_ready = sem("merged_ready")
        mix_ready = sem("mix_ready")
        lam_abs = sem("lam_abs")
        lam_exp = sem("lam_exp")
        lam_ready = sem("lam_ready")
        sig_ready = sem("sig_ready")
        decay_exp = sem("decay_exp")
        var_ready = sem("var_ready")
        var_root = sem("var_root")
        angle_ready = sem("angle_ready")
        sincos_ready = sem("sincos_ready")
        lat_ready = sem("lat_ready")
        head_ready = sem("head_ready")
        rope_ready = sem("rope_ready")
        stored = sem("stored")

        NORMS = 3

        wg = w["ffn_w_gate"].rearrange("l j (k p) f -> l j p k f", p=P)
        wu = w["ffn_w_up"].rearrange("l j (k p) f -> l j p k f", p=P)
        wd = w["ffn_w_down"].rearrange("l j (k p) d -> l j p k d", p=P)
        w_in = w["w_in"].rearrange("l (k p) n -> l p k n", p=P)
        w_br = w["w_branch"].rearrange("l b (k p) d -> l b p k d", p=P)
        w_out = w["w_out"].rearrange("l (k p) d -> l p k d", p=P)
        w_ada = w["w_ada"].rearrange("l (k p) n -> l p k n", p=P)
        cw_in = w["conv_w_in_2"].rearrange("l (k p) n -> l p k n", p=P)
        cw_out = w["conv_w_out_2"].rearrange("l (k p) n -> l p k n", p=P)
        rw_in = w["lru_w_in_2"].rearrange("l (k p) n -> l p k n", p=P)
        rw_out = w["lru_w_out_2"].rearrange("l (k p) n -> l p k n", p=P)
        rw_a = w["lru_gate_a_w_2"].rearrange("l n d e -> l d n e")
        rw_x = w["lru_gate_x_w_2"].rearrange("l n d e -> l d n e")
        mw_down = w["mla_w_down_2"].rearrange("l (k p) n -> l p k n", p=P)
        mw_uq = w["mla_w_uq_2"].rearrange("l (k p) n -> l p k n", p=P)
        mw_ukv = w["mla_w_ukv_2"].rearrange("l (k p) n -> l p k n", p=P)
        mw_o = w["mla_w_o_2"].rearrange("l (k p) n -> l p k n", p=P)
        w_gu = w["ffn_w_gu_2"].rearrange("l (k p) n -> l p k n", p=P)
        w_dn = w["ffn_w_down_2"].rearrange("l (k p) n -> l p k n", p=P)

        WIN_COL = {"u": lambda n: 3 * MIX_COLS + UC * n,
                   "qk": lambda n: (0 if n < 4 else 4 * MIX_COLS) + UC * (n % 4),
                   "v": lambda n: (2 * MIX_COLS if n < 2 else 6 * MIX_COLS) + UC * (n % 2)}

        def slot(u, nk, cols):
            return ring[:, u % SLOTS, 0:nk * cols].rearrange("p (k c) -> p k c", k=nk)

        STEPS = 2 * KT - 1

        def ada_count(l, j, k):
            if j < 2:
                return 7 * STEPS + (STEPS - 1) * j + 1 + 2 * k
            return at(l, 9 * STEPS - 2, STEPS * (j - 2) + 1 + 2 * k)

        def row_summed(eng, l, j):
            if j < 2:
                eng.wait_ge(first_rows, at(l, 2, j + 1))
            else:
                eng.wait_ge(ada_step, ada_count(l, j, KT - 1))

        def ffn_count(l, nf, per, n):
            return at(l, 2 * per, nf * per + n)

        def ffn_of(b, name):
            return name[0] if b else name[1]

        def ffn_shape(m):
            return KT if m < GU else THIRDS[(m - GU) % 3][1] - THIRDS[(m - GU) % 3][0]

        def high_count(b, l, first, m, t):
            return at(l, 2 * NS, 2 * (split_of[b][first] + m) + t + 1)

        def low_count(b, l, first, m):
            return at(l, 2 * NS, 2 * (split_of[b][first] + m + 1)) + 2 * SLOTS

        def norms_split(layer, ffn):
            return layer + layer // 3 + ffn

        def ffn_used(eng, l, nf, g0, m, i=0):
            if m < GU or (m - GU) % 3 == 2:
                eng.wait_ge(g_full, at(l, NG, g0 + (m if m < GU else GU + (m - GU) // 3) + 1) + 4 * i + 1)
            else:
                eng.wait_ge(down_part, ffn_count(l, nf, 8, 2 * ((m - GU) // 3) + (m - GU) % 3 + 1))

        def g_taken(eng, b, l, name):
            t = g_of[b][name]
            eng.wait_ge(g_free[t % BANKS], at(l, NG // BANKS, t // BANKS + 1) + 1)

        def m_taken(eng, b, l, name):
            t = m_of[b][name]
            eng.wait_ge(m_free[t % BANKS], at(l, NM // BANKS, t // BANKS + 1) + 1)

        block = ctx.enter_context(nc.Block())

        @block.sync
        def _(sp):
            def load(b, l, name, src):
                u = u_of[b][name]
                before = (U2 if b else U1)[u - SLOTS] if u >= SLOTS else None
                if before is None:
                    sp.wait_ge(w_low, at(l, 2 * NS, 2 * (u - SLOTS + 1)) + 2 * SLOTS)
                elif (b, before) in reader:
                    sp.wait_ge(g_full, at(l, NG, reader[b, before] + 1) + 1)
                else:
                    sp.wait_ge(w_low, low_count(b, l, before, 0))
                sp.dma_start(slot(u, src.shape[1], src.shape[2]), src).then_inc(unit_loaded[u % SLOTS], 16)

            def load_ffn(b, l, gate0, gate, up, down):
                u0 = u_of[b][gate0]
                name = (lambda what, j: gate0[:1] + (what, j)) if b else (lambda what, j: (what, gate0[1], j))
                for j in (0, 1):
                    load(b, l, name("gate", j), gate(j))
                    load(b, l, name("up", j), up(j))
                with sp.Fori(0, (GU - 4) // 4) as i:
                    for s in range(4):
                        j = sp.snap(2 * i + 2 + s // 2)
                        sp.wait_ge(w_low, low_count(b, l, gate0, s) + 8 * i)
                        sp.dma_start(slot(u0 + s, KT, UC), (gate, up)[s % 2](j)).then_inc(
                            unit_loaded[(u0 + s) % SLOTS], 16)
                for j in range(2 * ((GU - 4) // 4) + 2, FJ):
                    load(b, l, name("gate", j), gate(j))
                    load(b, l, name("up", j), up(j))
                for p in range(4):
                    for third, (k0, k1) in enumerate(THIRDS):
                        n = gate0[:1] + ("down", p, third) if b else ("down", gate0[1], p, third)
                        load(b, l, n, down(p, k0, k1))

            def cols(n):
                return bass.ds(UC * n, UC)

            def ffn1(l, n):
                load_ffn(0, l, ("gate", n, 0), lambda j: wg[l, n, :, :, cols(j)], lambda j: wu[l, n, :, :, cols(j)],
                         lambda p, k0, k1: wd[l, n, :, k0:k1, UC * p:UC * (p + 1)])

            sp.wait_ge(ada_first[KT - 2], 16)
            with sp.Fori(0, LAYERS1) as l:
                ffn1(l, 0)
                w_in_tiles = w["w_in"].rearrange("l (k p) n -> p (l k) n", p=P)
                w_br_tiles = w["w_branch"].rearrange("l b (k p) d -> p (l b k) d", p=P)
                for n in U1[u_of[0][("win", "u", 0)]:u_of[0][("gate", 1, 0)]]:
                    if n[0] == "win":
                        c = WIN_COL[n[1]](n[2])
                        src = w_in[l, :, :, c:c + UC] if c else w_in_tiles[:, bass.ds(l * KT, KT), 0:UC]
                    elif n[0] == "gates":
                        src = w_in[l, :, :, G_COL + UC * n[1]:G_COL + UC * (n[1] + 1)]
                    elif n[0] == "branch":
                        src = w_br[l, n[1], :, :, 2 * UC * n[2]:2 * UC * (n[2] + 1)]
                        if n[1:] == (0, 0):
                            src = w_br_tiles[:, bass.ds(l * 3 * (MIX_COLS // P), MIX_COLS // P), 0:2 * UC]
                    else:
                        src = w_out[l, :, :, UC * n[1]:UC * (n[1] + 1)]
                    load(0, l, n, src)
                ffn1(l, 1)

            L2 = LAYERS1
            for layer in range(LAYERS2):
                for n in U2:
                    if n[0] != layer or n[1] in ("gate", "up", "down"):
                        continue
                    if n[1] == "conv":
                        c = (D * (1 + n[2] // 4)) % (3 * D) + UC * (n[2] % 4)
                        src = cw_in[layer // 3, :, :, c:c + UC]
                    elif n[1] == "rec":
                        src = rw_in[0, :, :, LRU_W + UC * n[2]:LRU_W + UC * (n[2] + 1)]
                    elif n[1] == "gelu":
                        src = rw_in[0, :, :, UC * n[2]:UC * (n[2] + 1)]
                    elif n[1] == "blocks":
                        src = (rw_a, rw_x)[n[2]][0]
                    elif n[1] == "cdown":
                        src = mw_down[0, :, :, UC * n[2]:min(UC * (n[2] + 1), QL + KVL + ROPE)]
                    elif n[1] == "uq":
                        src = mw_uq[0, :, :, 768 * n[2]:768 * (n[2] + 1)]
                    elif n[1] == "ukv":
                        src = mw_ukv[0, :, :, D * n[2]:D * (n[2] + 1)]
                    else:
                        o = (cw_out[layer // 3], rw_out[0], mw_o[0])[layer % 3]
                        src = o[:, :, UC * n[2]:UC * (n[2] + 1)]
                    load(1, L2, n, src)
                load_ffn(1, L2, (layer, "gate", 0), lambda j: w_gu[layer, :, :, cols(j)],
                         lambda j: w_gu[layer, :, :, bass.ds(UC * j + F, UC)],
                         lambda p, k0, k1: w_dn[layer, :, k0:k1, UC * p:UC * (p + 1)])

            for p in range(4):
                g_taken(sp, 1, L2, (LAYERS2 - 1, "down", p))
                sp.dma_start(out[:, 2 * p:2 * p + 2, :], x[:, 2 * p:2 * p + 2, :]).then_inc(stored, 16)
            sp.wait_ge(stored, 64)

        @block.gpsimd
        def _(pool):
            def row_free(l, j):
                m_taken(pool, 0, l, ("mod", 0 if j == 1 else j))

            pool.wait_ge(unit_loaded[1], 16)
            pool.wait_ge(cact_ready, 1)
            pool.dma_start(cst[:, C_IDENT:C_ALL], w["constants"][:, C_IDENT:C_ALL]).then_inc(const_loaded, 16)
            pool.dma_start(v2[:, :], w["vectors_2"]).then_inc(const_loaded, 16)
            pool.dma_start(posi[:, :], w["positions_2"].partition_broadcast(ROPE)).then_inc(pos_loaded, 16)
            rows = [(l, j) for l in range(LAYERS1) for j in range(N_MOD)]
            for n, (l, j) in enumerate(rows[2:]):
                def fetch(k):
                    src = w_ada[l, :, k, D * j:D * (j + 1)]
                    pool.dma_start(ada_ring[:, k % 4, :], src).then_inc(ada_loaded[k % 4], 16)

                for k in range(4):
                    fetch(k)
                acc = ada_acc[:, j % 3, :]
                if l or j >= 3:
                    row_free(*rows[n + 2 - 3])
                for k in range(KT):
                    part = ada_ring[:, k % 4, :]
                    scale = cact[:, k:k + 1].to_broadcast([P, D])
                    last = first_rows if j < 2 and k == KT - 1 else ada_step
                    pool.wait_ge(ada_loaded[k % 4], 16 * (2 * n + k // 4 + 1))
                    pool.tensor_tensor(part if k else acc, part, scale, ALU.mult).then_inc(ada_step, 1)
                    if k:
                        pool.wait_ge(ada_step, ada_count(l, j, k) - 1)
                        pool.tensor_tensor(acc, acc, part, ALU.add).then_inc(last, 1)
                    if k < 4:
                        pool.wait_ge(ada_step, ada_count(l, j, k))
                        fetch(k + 4)
                row_summed(pool, l, j)
            for l, j in rows[-3:]:
                row_free(l, j)

        @block.tensor
        def _(pe):
            def open_g(b, l, name):
                t = g_of[b][name]
                pe.wait_ge(g_free[t % BANKS], at(l, NG // BANKS, t // BANKS) + 1)
                return gbank(t)

            def open_m(b, l, name):
                t = m_of[b][name]
                pe.wait_ge(m_free[t % BANKS], at(l, NM // BANKS, t // BANKS) + 1)
                return mbank(t)

            def unit(b, l, name, nk, cols):
                u = u_of[b][name]
                pe.wait_ge(unit_loaded[u % SLOTS], at(l, 16 * NU // SLOTS, 16 * (u // SLOTS + 1)))
                return slot(u, nk, cols)

            def tiles(bank, wt, rhs, n, hwait=None):
                nk = wt.shape[1]
                for t in range(n):
                    for k in range(nk):
                        if hwait and t == 0:
                            hwait(k)
                        mm = pe.matmul(two(bank)[:, t, :], wt[:, k, P * t:P * (t + 1)], rhs[:, k, :],
                                       start=(k == 0), stop=(k == nk - 1))
                return mm

            def mod_row(l, rows):
                bank = open_m(0, l, ("mod", rows[0]))
                for n, j in enumerate(rows):
                    row_summed(pe, l, j)
                    for c in range(KT):
                        mm = pe.matmul(bank[:, KT * n + c:KT * n + c + 1], ada_acc[:, j % 3, P * c:P * (c + 1)],
                                       ones[:, 0:1], start=True, stop=True)
                mm.then_inc(m_full, 1)

            def norm_sum(b, l, name, nn):
                bank = open_m(b, l, name)
                for n, sq in enumerate((sqacc, sqx)):
                    pe.wait_ge(x_ready, nn * 4 + 3 + n)
                    for t in range(2):
                        mm = pe.matmul(bank[:, 0:S], ones, sq[:, S * t:S * (t + 1)], start=(n == 0 and t == 0),
                                       stop=(n == 1 and t == 1))
                mm.then_inc(m_full, 1)

            def h_tile(nn):
                return lambda k: pe.wait_ge(h_ready, nn * KT + k + 1)

            def products(bank, m, x_r, t, k, first, last):
                wt = w_parts[:, m % 2, :, :].rearrange("p r (k c) -> p r k c", c=UC)
                for wi, xi in ((1, 0), (0, 1), (0, 0)):
                    mm = pe.matmul(bank[:, t, :], wt[:, wi, k, P * t:P * (t + 1)], x_r[:, xi, :],
                                   start=first and wi == 1, stop=last and (wi, xi) == (0, 0),
                                   skip_group_check=True)
                return mm

            def split(b, l, first, m, t, more=0):
                pe.wait_ge(w_low, low_count(b, l, first, m) - 1 + t + more)

            def split_unit(b, l, first, m, bank, x_r, more=0, xwait=None):
                for t in range(2):
                    split(b, l, first, m, t, more)
                    for k in range(KT):
                        if xwait and t == 0:
                            xwait(k)
                        mm = products(two(bank), m, x_r[:, :, k, :], t, k, k == 0, k == KT - 1)
                mm.then_inc(g_full, 1)

            def first_unit(b, l, first, nn):
                bank = two(open_g(b, l, first))
                split(b, l, first, 0, 1)
                for k in range(KT):
                    pe.wait_ge(h_ready, nn * KT + k + 1)
                    for t in range(2):
                        mm = products(bank, 0, h_r[:, :, k, :], t, k, k == 0 and t == 0, k == KT - 1)
                mm.then_inc(g_full, 1)

            def ffn(b, l, gate0, nn, between=None):
                g0, nf = g_of[b][gate0], ffn_of(b, gate0)

                first_unit(b, l, gate0, nn)
                split_unit(b, l, gate0, 1, open_g(b, l, (gate0[0], "up", 0) if b else ("up", gate0[1], 0)), h_r)
                with pe.Fori(0, (FJ - 1) // 2) as i:
                    for s in range(4):
                        g = g0 + 2 + s
                        pe.wait_ge(g_free[g % BANKS], at(l, NG // BANKS, g // BANKS) + i + 1)
                        split_unit(b, l, gate0, 2 + s, gbank(g), h_r, 8 * i)
                if between:
                    between()
                for p in range(4):
                    bank = two(open_g(b, l, (gate0[0], "down", p) if b else ("down", gate0[1], p)))
                    for third, (k0, k1) in enumerate(THIRDS):
                        m = GU + 3 * p + third
                        if p == 0:
                            pe.wait_ge(act_low, ffn_count(l, nf, FJ, k1 // 2) + 1)
                        for t in range(2):
                            split(b, l, gate0, m, t)
                            for k in range(k0, k1):
                                mm = products(bank, m, act_r[:, :, k, :], t, k - k0, k == 0 and t == 0, k == FT - 1)
                        mm.then_inc(g_full if third == 2 else down_part, 1)

            def qk_sum(l, n):
                bank = open_m(0, l, ("qk", n))
                g_taken(pe, 0, l, ("qk", n))
                pe.matmul(bank[:, :], halves, sqb[:, n % 2, :], start=True, stop=True).then_inc(m_full, 1)

            def scores(l, s):
                a, hd = s // HEADS, s % HEADS
                rows = slice(DH * (hd % 2), DH * (hd % 2) + DH)
                q, k = qk[rows, 8 * a + hd // 2, :], qk[rows, 8 * a + 4 + hd // 2, :]
                bank = open_m(0, l, ("s", s))
                pe.wait_ge(qk_ready, at(l, 8, 4 * a + 3 + (hd // 2) // 2))
                for lo, hi, keys in ((0, P, P), (P, 3 * P, S)):
                    mm = pe.matmul(bank[:, lo:hi], q[:, 0:P] if lo == 0 else q[:, P:S], k[:, 0:keys],
                                   start=True, stop=(a == 0))
                    if a:
                        if lo == 0 and hd == 0:
                            pe.wait_ge(decay_ready, at(l, 1, 1))
                        mm = pe.matmul(bank[:, lo:hi], cst[0:HEADS, C_SEL + P * hd:C_SEL + P * (hd + 1)],
                                       fz[0:HEADS, 0, 0:keys], start=False, stop=True)
                mm.then_inc(m_full, 1)

            def turn_probs(b, l, name, n, pr):
                bank = open_m(b, l, name)
                pe.wait_ge(prob_ready, n + 1)
                for i in range(3):
                    mm = pe.transpose(bank[:, P * i:P * (i + 1)], pr[:, P * i:P * (i + 1)], ident)
                mm.then_inc(m_full, 1)

            def values(b, l, name, turned, v0, v1, rows, pt):
                bank = open_m(b, l, name)
                m_taken(pe, b, l, turned)
                pe.matmul(bank[rows, 0:S], v0, pt[:, 0:S], start=True, stop=False)
                pe.matmul(bank[rows, P:S], v1, pt[:, S:3 * P], start=False, stop=True).then_inc(m_full, 1)

            def branch(l, n, u):
                wt = unit(0, l, ("branch", n, u), 4, 2 * UC)
                for i in range(2):
                    bank = open_g(0, l, ("branch", n, u, i))
                    tiles(bank, wt[:, :, UC * i:UC * (i + 1)], ybr[:, 4 * n:4 * n + 4, :], 2).then_inc(g_full, 1)

            pe.wait_ge(ones_loaded, 16)
            with pe.Fori(0, LAYERS1) as l:
                norm_sum(0, l, ("norm", 0), l * NORMS)
                mod_row(l, [0, 1])
                ffn(0, l, ("gate", 0, 0), l * NORMS, lambda: mod_row(l, [2]))
                pe.wait_ge(const_loaded, 32)
                mod_row(l, [3])
                mod_row(l, [4])
                norm_sum(0, l, ("norm", 1), l * NORMS + 1)
                for u in range(2):
                    wt = unit(0, l, ("win", "u", u), KT, UC)
                    tiles(open_g(0, l, ("u", u)), wt, h, 2, None if u else h_tile(l * NORMS + 1)).then_inc(g_full, 1)
                bank = open_m(0, l, "f")
                for k in range(KT):
                    mm = pe.matmul(bank[0:HEADS, 0:S], lv[:, L_WF + HEADS * k:L_WF + HEADS * (k + 1)], h[:, k, :],
                                   start=(k == 0), stop=(k == KT - 1))
                mm.then_inc(m_full, 1)
                for n in range(8):
                    wt = unit(0, l, ("win", "qk", n), KT, UC)
                    tiles(open_g(0, l, ("qk", n)), wt, h, 2).then_inc(g_full, 1)
                    if n:
                        qk_sum(l, n - 1)
                for n in range(4):
                    wt = unit(0, l, ("win", "v", n), KT, UC)
                    bank = two(open_g(0, l, ("v", n)))
                    for t in range(2):
                        for k in range(KT):
                            mm = pe.matmul(bank[:, t, :], h[:, k, P * t:P * (t + 1)], wt[:, k, :],
                                           start=(k == 0), stop=(k == KT - 1))
                    mm.then_inc(g_full, 1)
                    if n == 0:
                        qk_sum(l, 7)
                for n in range(2):
                    bank = two(open_g(0, l, ("pool", n)))
                    pe.wait_ge(diff_ready, at(l, 1, 1))
                    for t in range(2):
                        c = 2 * n + t
                        mm = pe.matmul(bank[:, t, :], lv[:, L_WP + P * c:L_WP + P * (c + 1)],
                                       win[:, 1, S * c:S * (c + 1)], start=True, stop=True)
                    mm.then_inc(g_full, 1)
                for i in range(ATT_STEPS):
                    if i < 2 * HEADS:
                        scores(l, i)
                    for what in STEP_UNITS.get(i, ()):
                        if what[0] == "gates":
                            wt = unit(0, l, what, KT, UC)
                            tiles(open_g(0, l, what), wt, h, 2).then_inc(g_full, 1)
                        else:
                            if what == ("branch", 1, 0):
                                g_taken(pe, 0, l, ("pool", 1))
                            if what == ("branch", 0, 0):
                                m_taken(pe, 0, l, ("pv", HEADS - 1))
                            branch(l, what[1], what[2])
                    if 0 <= i - 1 < 2 * HEADS:
                        turn_probs(0, l, ("pt", i - 1), at(l, 2 * HEADS, i - 1), prob[:, (i - 1) % 2, :])
                    if 0 <= i - 2 < 2 * HEADS:
                        s = i - 2
                        if s == 0:
                            g_taken(pe, 0, l, ("v", 3))
                        a, hd = s // HEADS, s % HEADS
                        c = slice(DH * hd, DH * (hd + 1))
                        values(0, l, ("pv", s), ("pt", s), vtok[:, a, 0, c], vtok[:, a, 1, c],
                               slice(DH * (hd % 2), DH * (hd % 2) + DH), probT[:, s % 2, :])
                m_taken(pe, 0, l, ("pv", 2 * HEADS - 1))
                for u in range(2):
                    branch(l, 2, u)
                mod_row(l, [5])
                for p in range(4):
                    wt = unit(0, l, ("wout", p), KT, UC)
                    bank = open_g(0, l, ("wout", p))
                    hw = None if p else (lambda k: pe.wait_ge(merged_ready, at(l, 4, k // 2 + 1)))
                    tiles(bank, wt, h, 2, hw).then_inc(g_full, 1)
                mod_row(l, [6])
                mod_row(l, [7])
                norm_sum(0, l, ("norm", 2), l * NORMS + 2)
                ffn(0, l, ("gate", 1, 0), l * NORMS + 2, lambda: mod_row(l, [8]))

            L2 = LAYERS1
            for layer in range(LAYERS2):
                nn = NORMS * LAYERS1 + 2 * layer
                norm_sum(1, L2, (layer, "norm", 0), nn)
                first = [h_tile(nn)]

                def plain(what, n):
                    for p in range(n):
                        wt = unit(1, L2, (layer, what, p), KT, UC)
                        tiles(open_g(1, L2, (layer, what, p)), wt, h, 2, first.pop() if first else None)\
                            .then_inc(g_full, 1)

                if layer % 3 == 0:
                    conv0 = (layer, "conv", 0)
                    first_unit(1, L2, conv0, nn)
                    for m in range(1, 12):
                        split_unit(1, L2, conv0, m, open_g(1, L2, (layer, "conv", m)), h_r)
                    for p in range(4):
                        xw = None if p else (lambda k: pe.wait_ge(y_low, 4 * (layer // 3) + k // 2 + 1))
                        split_unit(1, L2, conv0, 12 + p, open_g(1, L2, (layer, "out", p)), y_r, 0, xw)
                elif layer == 1:
                    plain("rec", 5)
                    wa = unit(1, L2, (1, "blocks", 0), LT, P)
                    wx = unit(1, L2, (1, "blocks", 1), LT, P)
                    for t in range(LT):
                        bank = two(open_g(1, L2, (1, "ri", t)))
                        pe.wait_ge(mix_ready, t + 1)
                        pe.matmul(bank[:, 0, :], wa[:, t, :], r_rec[:, t, :], start=True, stop=True)
                        pe.matmul(bank[:, 1, :], wx[:, t, :], r_rec[:, t, :], start=True, stop=True)\
                            .then_inc(g_full, 1)
                    plain("gelu", 5)
                    y, nk = r_g, LT
                else:
                    for p in range(3):
                        cols = UC if p < 2 else P + ROPE
                        wt = unit(1, L2, (2, "cdown", p), KT, cols)
                        bank = two(open_g(1, L2, (2, "cdown", p)))
                        hw = first.pop() if first else None
                        for t in range(2):
                            n = P if 2 * p + t < 5 else ROPE
                            for k in range(KT):
                                if hw and t == 0:
                                    hw(k)
                                mm = pe.matmul(bank[0:n, t, :], wt[:, k, P * t:P * t + n], h[:, k, :],
                                               start=(k == 0), stop=(k == KT - 1))
                        mm.then_inc(g_full, 1)
                    for name, lo, n, p, last in (("cq", 0, CQ, P, 1), ("ckv", CQ, CKV, P, 2), ("kr", 5, 1, ROPE, 2)):
                        bank = open_m(1, L2, (2, name))
                        g_taken(pe, 1, L2, (2, "cdown", last))
                        for k in range(n):
                            mm = pe.matmul(bank[0:p, 0:S], ones[0:p, 0:p], c_sq[0:p, lo + k, :],
                                           start=(k == 0), stop=(k == n - 1))
                        mm.then_inc(m_full, 1)
                    bank = open_m(1, L2, (2, "krot"))
                    pe.wait_ge(lat_ready, 3)
                    pe.matmul(bank[0:ROPE, 0:S], cst[0:ROPE, C_ROT:C_ROT + ROPE], c_lat[0:ROPE, 5, :],
                              start=True, stop=True).then_inc(m_full, 1)

                    def q_sum(hd):
                        bank = open_m(1, L2, (2, "qn", hd))
                        g_taken(pe, 1, L2, (2, "q", hd))
                        pe.matmul(bank[:, 0:S], ones, hsq[:, hd % 2, 0:S], start=True, stop=True)
                        pe.matmul(bank[0:ROPE, S:2 * S], ones[0:ROPE, 0:ROPE], hsq[0:ROPE, hd % 2, S:2 * S],
                                  start=True, stop=True).then_inc(m_full, 1)

                    def q_rot(hd):
                        bank = open_m(1, L2, (2, "qrot", hd))
                        pe.wait_ge(head_ready, hd + 1)
                        pe.matmul(bank[0:ROPE, 0:S], cst[0:ROPE, C_ROT:C_ROT + ROPE], qr[0:ROPE, hd, :],
                                  start=True, stop=True).then_inc(m_full, 1)

                    pe.wait_ge(lat_ready, 3)
                    for hd in range(HEADS):
                        wt = unit(1, L2, (2, "uq", hd // 4), CQ, 768)
                        bank = two(open_g(1, L2, (2, "q", hd)))
                        c = (NOPE + ROPE) * (hd % 4)
                        for t, (lo, n) in enumerate(((c, NOPE), (c + NOPE, ROPE))):
                            for k in range(CQ):
                                mm = pe.matmul(bank[0:n, t, :], wt[:, k, lo:lo + n], c_lat[:, k, :],
                                               start=(k == 0), stop=(k == CQ - 1))
                        mm.then_inc(g_full, 1)
                        if hd >= 1:
                            q_sum(hd - 1)
                        if hd >= 2:
                            q_rot(hd - 2)
                    wkv = [unit(1, L2, (2, "ukv", n), CKV, D) for n in range(2)]
                    for n in range(4):
                        t, grp = n % 2, n // 2
                        bank = open_g(1, L2, (2, "v", n))
                        for k in range(CKV):
                            vw = wkv[grp][:, k, :].rearrange("p (a c) -> p a c", a=4)[:, :, NOPE:NOPE + VD]
                            mm = pe.matmul(bank[:, :], c_lat[:, CQ + k, P * t:P * (t + 1)], vw,
                                           start=(k == 0), stop=(k == CKV - 1))
                        mm.then_inc(g_full, 1)
                    q_sum(HEADS - 1)
                    q_rot(HEADS - 2)
                    q_rot(HEADS - 1)
                    for hd in range(HEADS + 1):
                        if hd < HEADS:
                            bank = open_g(1, L2, (2, "k", hd))
                            for k in range(CKV):
                                lo = (NOPE + VD) * (hd % 4)
                                mm = pe.matmul(bank[:, 0:S], wkv[hd // 4][:, k, lo:lo + NOPE], c_lat[:, CQ + k, :],
                                               start=(k == 0), stop=(k == CKV - 1))
                            mm.then_inc(g_full, 1)
                        if hd >= 1:
                            bank = open_m(1, L2, (2, "kn", hd - 1))
                            g_taken(pe, 1, L2, (2, "k", hd - 1))
                            pe.matmul(bank[:, 0:S], ones, hsq[:, (hd - 1) % 2, 0:S], start=True, stop=True)\
                                .then_inc(m_full, 1)
                    pe.wait_ge(rope_ready, HEADS + 1)
                    for i in range(HEADS + 2):
                        if i < HEADS:
                            bank = open_m(1, L2, (2, "s", i))
                            pe.wait_ge(head_ready, HEADS + i + 1)
                            for lo, hi, keys in ((0, P, P), (P, 3 * P, S)):
                                qs = slice(0, P) if lo == 0 else slice(P, S)
                                pe.matmul(bank[:, lo:hi], qn[:, i, qs], kn[:, i, 0:keys], start=True, stop=False)
                                mm = pe.matmul(bank[:, lo:hi], qr[0:ROPE, i, qs], c_lat[0:ROPE, 5, 0:keys],
                                               start=False, stop=True)
                            mm.then_inc(m_full, 1)
                        if 0 <= i - 1 < HEADS:
                            turn_probs(1, L2, (2, "pt", i - 1), LAYERS1 * 2 * HEADS + i - 1, m_prob[:, (i - 1) % 2, :])
                        if 0 <= i - 2 < HEADS:
                            hd = i - 2
                            if hd == 0:
                                g_taken(pe, 1, L2, (2, "v", 3))
                            c = slice(VD * hd, VD * (hd + 1))
                            values(1, L2, (2, "pv", hd), (2, "pt", hd), mla_v[:, 0, c], mla_v[:, 1, c],
                                   slice(0, P), m_probT[:, hd % 2, :])
                    y, nk = mla_y, KT

                for p in range(4) if layer % 3 else ():
                    wt = unit(1, L2, (layer, "out", p), nk, UC)
                    bank = open_g(1, L2, (layer, "out", p))
                    if layer == 1:
                        hw = lambda k: pe.wait_ge(mix_ready, LT + k + 1)
                    else:
                        hw = lambda k: m_taken(pe, 1, L2, (2, "pv", k))
                    tiles(bank, wt, y, 2, None if p else hw).then_inc(g_full, 1)
                norm_sum(1, L2, (layer, "norm", 1), nn + 1)
                ffn(1, L2, (layer, "gate", 0), nn + 1)

        @block.scalar
        def _(act):
            def g_full_at(b, l, name):
                t = g_of[b][name]
                act.wait_ge(g_full, at(l, NG, t + 1) + 1)
                return gbank(t), g_free[t % BANKS]

            def m_full_at(b, l, name):
                t = m_of[b][name]
                act.wait_ge(m_full, at(l, NM, t + 1))
                return mbank(t), m_free[t % BANKS]

            def root(b, l, name):
                bank, free = m_full_at(b, l, name)
                act.activation(rs[:, 0:S], bank[:, 0:S], ACT.Sqrt, bias=eps, scale=1.0 / D).then_inc(free, 1)

            def add_shift(l, n, row):
                for k in range(KT):
                    act.wait_ge(h_scaled, (l * NORMS + n) * KT + k + 1)
                    act.activation(h[:, k, :], h[:, k, :], ACT.Identity,
                                   bias=mod[:, KT * row + k:KT * row + k + 1]).then_inc(h_ready, 1)

            def high_h(nn, bias):
                for k in range(KT):
                    act.wait_ge(h_scaled, nn * KT + k + 1)
                    if bias is None:
                        act.activation(h_r[:, 0, k, :], h[:, k, :], ACT.Copy).then_inc(h_high, 1)
                    else:
                        act.activation(h_r[:, 0, k, :], h[:, k, :], ACT.Identity,
                                       bias=mod[:, KT * bias + k:KT * bias + k + 1]).then_inc(h_high, 1)

            def high_part(l, u, m, nk, i=0):
                act.wait_ge(unit_loaded[u % SLOTS], at(l, 16 * NU // SLOTS, 16 * (u // SLOTS + 1)) + 16 * i)
                wt = w_parts[:, m % 2, 0, 0:nk * UC].rearrange("p (k c) -> p k c", c=UC)
                for t in range(2):
                    c = slice(P * t, P * (t + 1))
                    act.activation(wt[:, :, c], slot(u, nk, UC)[:, :, c], ACT.Copy).then_inc(w_high, 1)

            def conv_high_w(layer, m):
                if m >= 2:
                    act.wait_ge(g_full, at(LAYERS1, NG, g_of[1][(layer, "conv", 0)] + m - 1) + 1)
                elif layer:
                    ffn_used(act, LAYERS1, layer - 1, g_of[1][(layer - 1, "gate", 0)], FFN_UNITS - 2 + m)
                else:
                    ffn_used(act, LAYERS1 - 1, 1, g_of[0][("gate", 1, 0)], FFN_UNITS - 2 + m)
                high_part(LAYERS1, u_of[1][(layer, "conv", 0)] + m, m, KT)

            def high_w(b, l, gate0, m, i=0):
                if m >= 2:
                    ffn_used(act, l, ffn_of(b, gate0), g_of[b][gate0], m - 2, i)
                high_part(l, u_of[b][gate0] + m, m, ffn_shape(m), i)

            def first_high_w(b, l, gate0, after):
                t = g_of[b][after] + 1 if after else 0
                act.wait_ge(g_full, at(l, NG, t) + 1)
                for m in range(2):
                    high_w(b, l, gate0, m)

            def ffn(b, l, gate0):
                g0, nf = g_of[b][gate0], ffn_of(b, gate0)

                def pair(j, i):
                    g = g0 + 2 * j
                    high_w(b, l, gate0, 2 * j + 2, i)
                    act.wait_ge(g_full, at(l, NG, g + 1) + 4 * i + 1)
                    if j:
                        act.wait_ge(act_low, ffn_count(l, nf, FJ, j - 1) + 2 * i + 1)
                    act.activation(silu_g[:, j % 2, :], gbank(g)[:, :], ACT.Silu).then_inc(g_free[g % BANKS], 1)
                    high_w(b, l, gate0, 2 * j + 3, i)
                    act.wait_ge(g_free[(g + 1) % BANKS], at(l, NG // BANKS, (g + 1) // BANKS + 1) + i + 1)
                    act.activation(act_r[:, 0, bass.ds(2 * j + 4 * i, 2), :], tiled(silu_g[:, j % 2, :], 2), ACT.Copy)\
                        .then_inc(act_high, 1)

                pair(0, 0)
                with act.Fori(0, (FJ - 1) // 2) as i:
                    pair(1, i)
                    pair(2, i)
                for m in range(GU + 2, FFN_UNITS):
                    high_w(b, l, gate0, m)

            def exps(count, lg, pr, used):
                n, s = count
                act.wait_ge(max_ready, n + 1)
                if used is not None:
                    act.wait_ge(m_full, used)
                act.activation(pr[:, s, 0:P], lg[:, s, 0:P], ACT.Exp, bias=small[:, 6 * s:6 * s + 1],
                               accum_out=small[:, 6 * s + 2:6 * s + 3])
                act.activation(pr[:, s, P:3 * P], lg[:, s, P:3 * P], ACT.Exp, bias=small[:, 6 * s + 1:6 * s + 2],
                               accum_out=small[:, 6 * s + 3:6 * s + 4]).then_inc(exp_ready, 1)

            def copy_turned(b, l, i, pre, pt):
                bank, free = m_full_at(b, l, pre + ("pt", i))
                if i >= 2:
                    act.wait_ge(m_full, at(l, NM, m_of[b][pre + ("pv", i - 2)] + 1))
                act.activation(pt[:, i % 2, :], bank[:, 0:3 * P], ACT.Copy).then_inc(free, 1)

            act.dma_start(cact[:, :], w["c"]).then_inc(c_loaded, 16)
            act.dma_start(rel_pad[:, 0:REL - 1],
                          w["rel_bias"].rearrange("l h r -> (l h) r")[:, 1:REL]).then_inc(rel_loaded, 16)
            for k in range(KT):
                act.dma_start(ada_wide[:, k, :], w_ada[0, :, k, 0:2 * D]).then_inc(ada_first[k], 16)
                if k == 3:
                    act.dma_start(x[:, :, :], w["x"]).then_inc(x_loaded, 16)
            act.dma_start(cst[:, 0:C_IDENT], w["constants"][:, 0:C_IDENT]).then_inc(ones_loaded, 16)
            act.wait_ge(c_loaded, 16)
            act.activation(cact[:, :], cact[:, :], ACT.Silu).then_inc(cact_ready, 1)
            act.wait_ge(rel_padded, 1)
            act.dma_start(rel_rows[:, :], rel_pad).then_inc(rel_stored, 16)

            with act.Fori(0, LAYERS1) as l:
                act.wait_ge(x_ready, at(l, 12, 4))
                act.dma_start(lv[:, :], w["vectors_1"][l]).then_inc(lv_loaded, 16)
                act.wait_ge(rel_stored, 16)
                act.wait_ge(ones_loaded, 16)
                first_high_w(0, l, ("gate", 0, 0), None)
                root(0, l, ("norm", 0))
                high_h(l * NORMS, 0)
                ffn(0, l, ("gate", 0, 0))
                act.wait_ge(const_loaded, 32)
                root(0, l, ("norm", 1))
                act.dma_start(relb[:, :, :], bass.AP(rel_rows, l * (HEADS * EXT), [[1, P], [EXT, HEADS], [1, S]]))\
                    .then_inc(relb_loaded, 16)
                add_shift(l, 1, 3)
                for u in range(2):
                    bank, free = g_full_at(0, l, ("u", u))
                    act.activation(u_in[:, 2 * S * u:2 * S * (u + 1)], bank[:, :], ACT.Copy).then_inc(free, 1)

                def qk_root_of(n):
                    bank, free = m_full_at(0, l, ("qk", n))
                    act.activation(sqb[:, n % 2, :], bank[:, :], ACT.Sqrt, bias=eps, scale=1.0 / DH).then_inc(free, 1)

                for n in range(8):
                    bank, free = g_full_at(0, l, ("qk", n))
                    if n >= 2:
                        act.wait_ge(qk_ready, at(l, 8, n - 1))
                    act.activation(qk[:, 2 * n:2 * n + 2, :], two(bank), ACT.Copy)
                    act.activation(sqb[:, n % 2, :], bank[:, :], ACT.Square).then_inc(free, 1)
                    if n == 0:
                        act.wait_ge(f_abs, at(l, 1, 1))
                        act.activation(fz[0:HEADS, 3, :], fz[0:HEADS, 2, :], ACT.Exp, scale=-1.0).then_inc(f_exp, 1)
                    else:
                        qk_root_of(n - 1)
                for n in range(4):
                    bank, free = g_full_at(0, l, ("v", n))
                    act.activation(vtok[:, n // 2, :, UC * (n % 2):UC * (n % 2 + 1)], two(bank), ACT.Copy)\
                        .then_inc(free, 1)
                    if n == 0:
                        qk_root_of(7)
                for n in range(2):
                    bank, free = g_full_at(0, l, ("pool", n))
                    for t in range(2):
                        c = 2 * n + t
                        ins = act.activation(ybr[:, 4 + c, :], two(bank)[:, t, :], ACT.Copy,
                                             scale=lv[:, L_PS + c:L_PS + c + 1])
                    ins.then_inc(free, 1)
                for i in range(ATT_STEPS):
                    if i < 2 * HEADS:
                        used = at(l, NM, m_of[0][("pt", i - 2)] + 1) if i >= 2 else None
                        exps((at(l, 2 * HEADS, i), i % 2), logit, prob, used)
                    for what in STEP_UNITS.get(i, ()):
                        if what[0] == "gates":
                            bank, free = g_full_at(0, l, what)
                            n = what[1]
                            act.activation(gates[:, 2 * n:2 * n + 2, :], two(bank), ACT.Exp, scale=-1.0)\
                                .then_inc(free, 1)
                    if 0 <= i - 1 < 2 * HEADS:
                        copy_turned(0, l, i - 1, (), probT)
                    if 0 <= i - 2 < 2 * HEADS:
                        s = i - 2
                        bank, free = m_full_at(0, l, ("pv", s))
                        rows = slice(DH * (s % 2), DH * (s % 2) + DH)
                        y_tile = 8 * (s // HEADS) + (s % HEADS) // 2
                        act.activation(ybr[rows, y_tile, :], bank[rows, 0:S], ACT.Copy).then_inc(free, 1)
                first_high_w(0, l, ("gate", 1, 0), ("wout", 0))
                root(0, l, ("norm", 2))
                high_h(l * NORMS + 2, 6)
                ffn(0, l, ("gate", 1, 0))

            L2 = LAYERS1
            for layer in range(LAYERS2):
                if layer % 3 == 0:
                    conv_high_w(layer, 0)
                    conv_high_w(layer, 1)
                root(1, L2, (layer, "norm", 0))
                if layer % 3 == 0:
                    high_h(NORMS * LAYERS1 + norms_split(layer, 0), None)
                    for m in range(14):
                        conv_high_w(layer, m + 2)
                        if m < 4:
                            bank, free = g_full_at(1, L2, (layer, "conv", m))
                            act.activation(cv_c[:, 2 * m:2 * m + 2, :], two(bank), ACT.Copy).then_inc(free, 1)
                        elif 8 <= m < 12:
                            g_taken(act, 1, L2, (layer, "conv", m))
                            pair = slice(2 * (m - 8), 2 * (m - 8) + 2)
                            act.activation(y_r[:, 0, pair, :], mix_y[:, pair, :], ACT.Copy).then_inc(y_high, 1)
                elif layer == 1:
                    act.wait_ge(lam_abs, 1)
                    act.activation(lamb[:, 3, :], lamb[:, 2, :], ACT.Exp, scale=-1.0).then_inc(lam_exp, 1)
                    for p in range(5):
                        bank, free = g_full_at(1, L2, (1, "rec", p))
                        act.activation(r_raw[:, 2 * p:2 * p + 2, :], two(bank), ACT.Copy).then_inc(free, 1)
                    for t in range(LT):
                        bank, free = g_full_at(1, L2, (1, "ri", t))
                        act.activation(r_r[:, t, :], bank[:, 0:S], ACT.Sigmoid, bias=v2[:, V_LAB + t:V_LAB + t + 1])\
                            .then_inc(sig_ready, 1)
                        act.activation(r_i[:, t, :], bank[:, S:2 * S], ACT.Sigmoid,
                                       bias=v2[:, V_LXB + t:V_LXB + t + 1]).then_inc(free, 1)
                    act.wait_ge(lam_ready, 1)
                    act.wait_ge(sig_ready, LT)
                    for t in range(LT):
                        act.activation(r_a[:, t, :], r_r[:, t, :], ACT.Exp, scale=lam8[:, t:t + 1])
                        act.activation(r_t[:, t, :], r_r[:, t, :], ACT.Tanh, scale=lam8[:, LT + t:LT + t + 1])\
                            .then_inc(decay_exp, 1)
                    for n in range(2):
                        act.wait_ge(var_ready, n + 1)
                        act.activation(r_t[:, 5 * n:5 * n + 5, :], r_t[:, 5 * n:5 * n + 5, :], ACT.Sqrt)\
                            .then_inc(var_root, 1)
                    for p in range(5):
                        bank, free = g_full_at(1, L2, (1, "gelu", p))
                        act.activation(r_g[:, 2 * p:2 * p + 2, :], two(bank), ACT.Gelu_apprx_tanh).then_inc(free, 1)
                else:
                    for n in range(2):
                        act.wait_ge(angle_ready, n + 1)
                        act.activation((cosT, sinT)[n][0:ROPE, :], (cosT, sinT)[n][0:ROPE, :], ACT.Sin)\
                            .then_inc(sincos_ready, 1)
                    for n in range(3):
                        bank, free = g_full_at(1, L2, (2, "cdown", n))
                        if n < 2:
                            act.activation(c_lat[:, 2 * n:2 * n + 2, :], two(bank), ACT.Copy)
                            act.activation(c_sq[:, 2 * n:2 * n + 2, :], two(bank), ACT.Square).then_inc(free, 1)
                        else:
                            act.activation(c_lat[:, 4, :], bank[:, 0:S], ACT.Copy)
                            act.activation(c_lat[0:ROPE, 5, :], bank[0:ROPE, S:2 * S], ACT.Copy)
                            act.activation(c_sq[:, 4, :], bank[:, 0:S], ACT.Square)
                            act.activation(c_sq[0:ROPE, 5, :], bank[0:ROPE, S:2 * S], ACT.Square).then_inc(free, 1)
                    for i, (name, n, rows) in enumerate((("cq", QL, P), ("ckv", KVL, P), ("kr", ROPE, ROPE))):
                        bank, free = m_full_at(1, L2, (2, name))
                        act.activation(lroot[0:rows, i, :], bank[0:rows, 0:S], ACT.Sqrt, bias=eps[0:rows, :],
                                       scale=1.0 / n).then_inc(free, 1)

                    def q_root(hd):
                        bank, free = m_full_at(1, L2, (2, "qn", hd))
                        act.activation(hsq[:, hd % 2, 0:S], bank[:, 0:S], ACT.Sqrt, bias=eps, scale=1.0 / NOPE)
                        act.activation(hsq[0:ROPE, hd % 2, S:2 * S], bank[0:ROPE, S:2 * S], ACT.Sqrt,
                                       bias=eps[0:ROPE, :], scale=1.0 / ROPE).then_inc(free, 1)

                    for hd in range(HEADS):
                        bank, free = g_full_at(1, L2, (2, "q", hd))
                        if hd >= 2:
                            act.wait_ge(head_ready, hd - 1)
                        act.activation(qn[:, hd, :], bank[:, 0:S], ACT.Copy)
                        act.activation(qr[0:ROPE, hd, :], bank[0:ROPE, S:2 * S], ACT.Copy)
                        act.activation(hsq[:, hd % 2, 0:S], bank[:, 0:S], ACT.Square)
                        act.activation(hsq[0:ROPE, hd % 2, S:2 * S], bank[0:ROPE, S:2 * S], ACT.Square)\
                            .then_inc(free, 1)
                        if hd >= 1:
                            q_root(hd - 1)
                    for n in range(4):
                        bank, free = g_full_at(1, L2, (2, "v", n))
                        act.activation(mla_v[:, n % 2, 4 * VD * (n // 2):4 * VD * (n // 2 + 1)], bank[:, :], ACT.Copy)\
                            .then_inc(free, 1)
                    q_root(HEADS - 1)
                    for hd in range(HEADS + 1):
                        if hd < HEADS:
                            bank, free = g_full_at(1, L2, (2, "k", hd))
                            act.wait_ge(head_ready, HEADS + hd - 1)
                            act.activation(kn[:, hd, :], bank[:, 0:S], ACT.Copy)
                            act.activation(hsq[:, hd % 2, 0:S], bank[:, 0:S], ACT.Square).then_inc(free, 1)
                        if hd >= 1:
                            bank, free = m_full_at(1, L2, (2, "kn", hd - 1))
                            act.activation(hsq[:, (hd - 1) % 2, 0:S], bank[:, 0:S], ACT.Sqrt, bias=eps,
                                           scale=1.0 / NOPE).then_inc(free, 1)
                    for i in range(HEADS + 2):
                        if i < HEADS:
                            used = at(L2, NM, m_of[1][(2, "pt", i - 2)] + 1) if i >= 2 else None
                            exps((2 * HEADS * LAYERS1 + i, i % 2), m_logit, m_prob, used)
                        if 0 <= i - 1 < HEADS:
                            copy_turned(1, L2, i - 1, (2,), m_probT)
                        if 0 <= i - 2 < HEADS:
                            bank, free = m_full_at(1, L2, (2, "pv", i - 2))
                            act.activation(mla_y[:, i - 2, :], bank[:, 0:S], ACT.Copy).then_inc(free, 1)
                for m in range(2):
                    g_full_at(1, L2, (layer, "out", 0 if layer % 3 else 2 + m))
                    high_w(1, L2, (layer, "gate", 0), m)
                root(1, L2, (layer, "norm", 1))
                high_h(NORMS * LAYERS1 + norms_split(layer, 1), None)
                ffn(1, L2, (layer, "gate", 0))

        @block.vector
        def _(dve):
            done = [0]
            for n, free in enumerate(g_free + m_free + [g_full, act_low, w_low]):
                dve.memset(opened[:, n:n + 1], 0.0).then_inc(free, 2 * SLOTS if free is w_low else 1)
            base = [0]

            def step(ins):
                done[0] += 1
                ins.then_inc(dve_step, 1)

            def settle(l):
                dve.wait_ge(dve_step, base[0] + at(l, DVE_PER, done[0]))

            def g_full_at(b, l, name):
                t = g_of[b][name]
                dve.wait_ge(g_full, at(l, NG, t + 1) + 1)
                return gbank(t), g_free[t % BANKS]

            def m_full_at(b, l, name):
                t = m_of[b][name]
                dve.wait_ge(m_full, at(l, NM, t + 1))
                return mbank(t), m_free[t % BANKS]

            def squares(l, p, stage):
                xp = x[:, 2 * p:2 * p + 2, :]
                if p == 0:
                    dve.tensor_tensor(tiled(sqacc[:, :], 2), xp, xp, ALU.mult).then_inc(x_ready, 1)
                    return
                dve.wait_ge(x_ready, stage * 4 + p)
                if p == 3:
                    dve.tensor_tensor(tiled(sqx[:, :], 2), xp, xp, ALU.mult).then_inc(x_ready, 1)
                    return
                step(dve.tensor_tensor(tiled(sqx[:, :], 2), xp, xp, ALU.mult))
                settle(l)
                dve.tensor_tensor(sqacc[:, :], sqacc[:, :], sqx[:, :], ALU.add).then_inc(x_ready, 1)

            def residual(b, l, names, gate, stage, last=False, before=None, after=None):
                for p, name in enumerate(names):
                    if before:
                        before(p)
                    bank, free = g_full_at(b, l, name)
                    if gate is None:
                        dve.tensor_tensor(x[:, 2 * p:2 * p + 2, :], two(bank), x[:, 2 * p:2 * p + 2, :], ALU.add)\
                            .then_inc(free, 1)
                    else:
                        for t in range(2):
                            k = 2 * p + t
                            ins = dve.scalar_tensor_tensor(out=x[:, k, :], in0=two(bank)[:, t, :],
                                                           scalar=gate[:, k:k + 1], in1=x[:, k, :],
                                                           op0=ALU.mult, op1=ALU.add)
                            if t:
                                ins.then_inc(free, 1)
                            else:
                                step(ins)
                    if not last:
                        g_taken(dve, b, l, name)
                        settle(l)
                        squares(l, p, stage)
                    if after:
                        after(p)

            def low_first(b, l, gate0):
                def after(p):
                    if p == 2:
                        for m in range(2):
                            low_w(b, l, gate0, m)
                return after

            def norm(b, l, name, gain, out_sem, low=None):
                m_taken(dve, b, l, name)
                step(dve.reciprocal(rs[:, S:2 * S], rs[:, 0:S]))
                if callable(gain):
                    gain = gain()
                settle(l)
                for k in range(KT + 2):
                    if k < KT:
                        dve.scalar_tensor_tensor(out=h[:, k, :], in0=x[:, k, :], scalar=gain[:, k:k + 1],
                                                 in1=rs[:, S:2 * S], op0=ALU.mult, op1=ALU.mult).then_inc(out_sem, 1)
                    if low and k >= 2:
                        low_h(l, low[0], k - 2, low[1])

            def low_h(l, n, k, shift):
                dve.wait_ge(h_high, ffn_count(l, n, KT, k + 1))
                if shift is None:
                    dve.tensor_tensor(h_r[:, 1, k, :], h[:, k, :], h_r[:, 0, k, :], ALU.subtract).then_inc(h_ready, 1)
                else:
                    dve.scalar_tensor_tensor(out=h_r[:, 1, k, :], in0=h[:, k, :], in1=h_r[:, 0, k, :],
                                             scalar=mod[:, KT * shift + k:KT * shift + k + 1],
                                             op0=ALU.add, op1=ALU.subtract).then_inc(h_ready, 1)

            def low_w(b, l, gate0, m, i=0):
                low_part(b, l, gate0, m, ffn_shape(m), i)

            def low_part(b, l, first, m, nk, i=0):
                u = u_of[b][first] + m
                wt = w_parts[:, m % 2, :, 0:nk * UC].rearrange("p r (k c) -> p r k c", c=UC)
                for t in range(2):
                    c = slice(P * t, P * (t + 1))
                    dve.wait_ge(w_high, high_count(b, l, first, m, t) + 8 * i)
                    dve.tensor_tensor(wt[:, 1, :, c], slot(u, nk, UC)[:, :, c], wt[:, 0, :, c], ALU.subtract)\
                        .then_inc(w_low, 1)

            def conv_low_w(layer, m):
                low_part(1, LAYERS1, (layer, "conv", 0), m, KT)

            def ffn(b, l, gate0, mods, gate, stage, last=False, conv=None):
                g0, nf = g_of[b][gate0], ffn_of(b, gate0)

                def pair(j, i):
                    g = g0 + 2 * j
                    low_w(b, l, gate0, 2 * j + 2, i)
                    dve.wait_ge(g_full, at(l, NG, g + 2) + 4 * i + 1)
                    dve.wait_ge(g_free[g % BANKS], at(l, NG // BANKS, g // BANKS + 1) + i + 1)
                    dve.tensor_tensor(silu_g[:, j % 2, :], gbank(g + 1)[:, :], silu_g[:, j % 2, :], ALU.mult)\
                        .then_inc(g_free[(g + 1) % BANKS], 1)
                    low_w(b, l, gate0, 2 * j + 3, i)
                    dve.wait_ge(act_high, ffn_count(l, nf, FJ, j + 1) + 2 * i)
                    c = bass.ds(2 * j + 4 * i, 2)
                    dve.tensor_tensor(act_r[:, 1, c, :], tiled(silu_g[:, j % 2, :], 2), act_r[:, 0, c, :],
                                      ALU.subtract).then_inc(act_low, 1)

                pair(0, 0)
                with dve.Fori(0, (FJ - 1) // 2) as i:
                    pair(1, i)
                    pair(2, i)
                if mods is not None:
                    mod_rows(l, mods, 1)
                    halve(l, mods)

                def split_down(p):
                    for m in range(GU + 3 * p + 2, min(GU + 3 * p + 5, FFN_UNITS)):
                        low_w(b, l, gate0, m)
                    if p == 3 and conv is not None:
                        conv_low_w(conv, 0)

                names = [(gate0[0], "down", p) if b else ("down", gate0[1], p) for p in range(4)]
                residual(b, l, names, gate, stage, last, split_down)

            def mod_rows(l, row, n):
                bank, free = m_full_at(0, l, ("mod", row))
                c = slice(KT * row, KT * (row + n))
                dve.tensor_tensor(mod[:, c], bank[:, 0:KT * n], lv[:, L_BADA + KT * row:L_BADA + KT * (row + n)],
                                  ALU.add).then_inc(free, 1)
                m_taken(dve, 0, l, ("mod", row))

            def gain_of(l, n, row):
                c = slice(KT * n, KT * (n + 1))
                step(dve.scalar_tensor_tensor(out=gains[:, c], in0=mod[:, KT * row:KT * (row + 1)], scalar=1.0,
                                              in1=lv[:, L_GAIN + KT * n:L_GAIN + KT * (n + 1)],
                                              op0=ALU.add, op1=ALU.mult))
                settle(l)
                return gains[:, c]

            def halve(l, row):
                c = slice(KT * row, KT * (row + 1))
                step(dve.tensor_scalar(mod[:, c], mod[:, c], 0.5, None, ALU.mult))
                settle(l)

            def magnitude(z, az, ready):
                dve.scalar_tensor_tensor(out=az, in0=z, scalar=-1.0, in1=z, op0=ALU.mult, op1=ALU.max)\
                    .then_inc(ready, 1)

            def softplus_neg(l, z, e, q, q2, p, t):
                def then(ins):
                    step(ins)
                    settle(l)

                then(dve.tensor_scalar(q, e, 2.0, None, ALU.add))
                then(dve.reciprocal(q2, q))
                then(dve.tensor_tensor(q, e, q2, ALU.mult))
                then(dve.tensor_tensor(q2, q, q, ALU.mult))
                then(dve.tensor_scalar(p, q2, 1.0 / 17, None, ALU.mult))
                for k in range(7, 0, -1):
                    then(dve.scalar_tensor_tensor(out=p, in0=p, scalar=1.0 / (2 * k + 1), in1=q2,
                                                  op0=ALU.add, op1=ALU.mult))
                then(dve.scalar_tensor_tensor(out=p, in0=p, scalar=1.0, in1=q, op0=ALU.add, op1=ALU.mult))
                then(dve.tensor_scalar(q, z, -1.0, 0.0, ALU.mult, ALU.max))
                return dve.scalar_tensor_tensor(out=t, in0=p, scalar=2.0, in1=q, op0=ALU.mult, op1=ALU.add)

            def soft_max(b, l, name, n, s, lg, bias0, bias1, slot_read):
                bank, free = m_full_at(b, l, name)
                if slot_read:
                    dve.wait_ge(exp_ready, n - 1)
                dve.memset(small[:, 12:13], 0.0)
                c = 6 * s
                step(dve.tensor_tensor_reduce(out=lg[:, s, 0:P], in0=bank[:, 0:P], in1=bias0, scale=1.0,
                                              scalar=-3e38, op0=ALU.add, op1=ALU.max,
                                              accum_out=small[:, 14 + c // 3:15 + c // 3]))
                dve.tensor_tensor_reduce(out=lg[:, s, P:3 * P], in0=bank[:, P:3 * P], in1=bias1, scale=1.0,
                                         scalar=-3e38, op0=ALU.add, op1=ALU.max,
                                         accum_out=small[:, 15 + c // 3:16 + c // 3]).then_inc(free, 1)
                m_taken(dve, b, l, name)
                settle(l)
                dve.tensor_scalar(small[:, c:c + 2], small[:, 14 + c // 3:16 + c // 3], -1.0, None, ALU.mult)\
                    .then_inc(max_ready, 1)

            def soft_norm(l, n, s, pr):
                c = 6 * s
                dve.wait_ge(exp_ready, n + 1)
                step(dve.reciprocal(small[:, c + 4:c + 6], small[:, c + 2:c + 4]))
                settle(l)
                step(dve.tensor_scalar(pr[:, s, 0:P], pr[:, s, 0:P], small[:, c + 4:c + 5], None, ALU.mult))
                dve.tensor_scalar(pr[:, s, P:3 * P], pr[:, s, P:3 * P], small[:, c + 5:c + 6], None, ALU.mult)\
                    .then_inc(prob_ready, 1)

            def merge(l, what):
                _, n, u = what
                for i in range(2):
                    bank, free = g_full_at(0, l, what + (i,))
                    pp = 2 * u + i
                    gate = gates[:, 8 * n + 2 * pp:8 * n + 2 * pp + 2, :]
                    settle(l)
                    if n == 1:
                        dve.tensor_tensor(h[:, 2 * pp:2 * pp + 2, :], two(bank), gate, ALU.mult).then_inc(free, 1)
                        continue
                    if n == 2 and (u or i):
                        dve.wait_ge(merged_ready, at(l, 4, pp))
                    dve.tensor_tensor(tiled(sqx[:, :], 2), two(bank), gate, ALU.mult).then_inc(free, 1)
                    g_taken(dve, 0, l, what + (i,))
                    if n == 0:
                        g_taken(dve, 0, l, ("branch", 1, u, i))
                    ins = dve.tensor_tensor(h[:, 2 * pp:2 * pp + 2, :], h[:, 2 * pp:2 * pp + 2, :],
                                            tiled(sqx[:, :], 2), ALU.add)
                    if n == 2:
                        ins.then_inc(merged_ready, 1)
                    else:
                        step(ins)

            dve.wait_ge(rel_loaded, 16)
            dve.tensor_copy(rel_pad[:, REL - 1:EXT],
                            rel_pad[:, REL - 2:REL - 1].to_broadcast([LAYERS1 * HEADS, EXT - REL + 1]))\
                .then_inc(rel_padded, 1)

            dve.wait_ge(cact_ready, 1)
            rows01 = ada_acc[:, 0:2, :].rearrange("p r d -> p (r d)")
            for k in range(KT):
                if k == 4:
                    dve.wait_ge(x_loaded, 16)
                    for p in range(4):
                        squares(0, p, 0)
                dve.wait_ge(ada_first[k], 16)
                if k == 0:
                    step(dve.tensor_scalar(rows01, ada_wide[:, 0, :], cact[:, 0:1], None, ALU.mult))
                    continue
                settle(0)
                if k < KT - 1:
                    step(dve.scalar_tensor_tensor(out=rows01, in0=ada_wide[:, k, :], scalar=cact[:, k:k + 1],
                                                  in1=rows01, op0=ALU.mult, op1=ALU.add))
                else:
                    dve.scalar_tensor_tensor(out=rows01, in0=ada_wide[:, k, :], scalar=cact[:, k:k + 1],
                                             in1=rows01, op0=ALU.mult, op1=ALU.add).then_inc(first_rows, 2)
            base[0], done[0] = done[0], 0

            with dve.Fori(0, LAYERS1) as l:
                for m in range(2):
                    low_w(0, l, ("gate", 0, 0), m)

                def first_gain():
                    dve.wait_ge(lv_loaded, at(l, 16, 16))
                    mod_rows(l, 0, 2)
                    return gain_of(l, 0, 1)

                norm(0, l, ("norm", 0), first_gain, h_scaled, (0, 0))
                ffn(0, l, ("gate", 0, 0), 2, mod[:, 2 * KT:3 * KT], l * 3 + 1)

                dve.wait_ge(const_loaded, 32)
                mod_rows(l, 3, 1)
                mod_rows(l, 4, 1)
                step(dve.tensor_scalar(qgain[:, 0:4:2], lv[:, L_QK:L_QK + 4:2], DH ** -0.5, None, ALU.mult))
                step(dve.tensor_copy(qgain[:, 1:4:2], lv[:, L_QK + 1:L_QK + 4:2]))
                norm(0, l, ("norm", 1), gain_of(l, 1, 4), h_scaled)

                bank, free = m_full_at(0, l, "f")
                z, az, e, q, q2, pl, sp_z = (fz[0:HEADS, n, :] for n in range(1, 8))
                dve.tensor_scalar(z, bank[0:HEADS, 0:S], lv[0:HEADS, L_FB:L_FB + 1], None, ALU.add).then_inc(free, 1)
                m_taken(dve, 0, l, "f")
                magnitude(z, az, f_abs)

                g_taken(dve, 0, l, ("u", 1))
                src = tiled(u_in, 4)
                bufs = [tiled(win[:, n, :], 4) for n in range(2)]
                for n in range(4):
                    sh, dst = 1 << n, bufs[n % 2]
                    step(dve.tensor_copy(dst[:, n:4, 0:sh], src[:, n:4, 0:sh]))
                    step(dve.tensor_tensor(dst[:, n:4, sh:S], src[:, n:4, sh:S], src[:, n:4, 0:S - sh], ALU.add))
                    settle(l)
                    src = dst
                for n in range(2):
                    step(dve.tensor_tensor(bufs[1][:, n:4:2, :], bufs[n][:, n:4:2, :], inv_count[:, n:4:2, :],
                                           ALU.mult))
                settle(l)
                dve.tensor_tensor(win[:, 1, :], win[:, 1, :], u_in, ALU.subtract).then_inc(diff_ready, 1)

                dve.wait_ge(f_exp, at(l, 1, 1))
                step(softplus_neg(l, z, e, q, q2, pl, sp_z))
                settle(l)
                dve.tensor_tensor_scan(out=fz[0:HEADS, 0, :], data0=ones_row[0:HEADS, :], data1=sp_z, initial=0.0,
                                       op0=ALU.mult, op1=ALU.add).then_inc(decay_ready, 1)

                for n in range(8):
                    m_taken(dve, 0, l, ("qk", n))
                    step(dve.reciprocal(sqb[:, n % 2, :], sqb[:, n % 2, :]))
                    settle(l)
                    dve.scalar_tensor_tensor(out=qk[:, 2 * n:2 * n + 2, :], in0=qk[:, 2 * n:2 * n + 2, :],
                                             scalar=qgain[:, n // 2:n // 2 + 1], in1=tiled(sqb[:, n % 2, :], 2),
                                             op0=ALU.mult, op1=ALU.mult).then_inc(qk_ready, 1)
                dve.wait_ge(relb_loaded, at(l, 16, 16))
                step(dve.memset(relb[0:CHUNK, :, 0:CHUNK], NEG))
                settle(l)

                for i in range(ATT_STEPS):
                    if i < 2 * HEADS:
                        a, hd = i // HEADS, i % HEADS
                        n = at(l, 2 * HEADS, i)
                        if a:
                            b0, b1 = causal[:, P:S], causal
                        else:
                            b0, b1 = relb[:, hd, 0:P][:, ::-1], relb[:, hd, :][:, ::-1]
                        soft_max(0, l, ("s", i), n, i % 2, logit, b0, b1, i >= 2)
                        soft_norm(l, n, i % 2, prob)
                    for what in STEP_UNITS.get(i, ()):
                        if what[0] == "gates":
                            g_taken(dve, 0, l, what)
                            gt = gates[:, 2 * what[1]:2 * what[1] + 2, :]
                            step(dve.tensor_scalar(gt, gt, 1.0, None, ALU.add))
                            settle(l)
                            step(dve.reciprocal(gt, gt))
                        else:
                            merge(l, what)
                for u in range(2):
                    merge(l, ("branch", 2, u))
                mod_rows(l, 5, 1)
                residual(0, l, [("wout", p) for p in range(4)], mod[:, 5 * KT:6 * KT], l * 3 + 2,
                         after=low_first(0, l, ("gate", 1, 0)))

                mod_rows(l, 6, 1)
                mod_rows(l, 7, 1)
                norm(0, l, ("norm", 2), gain_of(l, 2, 7), h_scaled, (1, 6))
                ffn(0, l, ("gate", 1, 0), 8, mod[:, 8 * KT:9 * KT], l * 3 + 3)
                assert done[0] == DVE_PER, done

            done[0] = 0
            L2 = LAYERS1

            def then(ins):
                step(ins)
                settle(L2)

            def causal_conv(src, dst, taps, bias, ready=None):
                if bias is None:
                    then(dve.tensor_scalar(dst, src, taps[0], None, ALU.mult))
                else:
                    then(dve.tensor_scalar(dst, src, taps[0], bias, ALU.mult, ALU.add))
                for lag in range(1, len(taps)):
                    ins = dve.scalar_tensor_tensor(out=dst[:, lag:S], in0=src[:, 0:S - lag], scalar=taps[lag],
                                                   in1=dst[:, lag:S], op0=ALU.mult, op1=ALU.add)
                    if ready is not None and lag == len(taps) - 1:
                        ins.then_inc(ready, 1)
                    else:
                        then(ins)

            def conv_mixer(layer):
                j = layer // 3
                for m in range(2, 6):
                    conv_low_w(layer, m)
                for p in range(4):
                    conv_low_w(layer, 6 + p)
                    g_taken(dve, 1, L2, (layer, "conv", p))
                    bank, free = g_full_at(1, L2, (layer, "conv", 4 + p))
                    pair = slice(2 * p, 2 * p + 2)
                    dve.tensor_tensor(cv_c[:, pair, :], two(bank), cv_c[:, pair, :], ALU.mult).then_inc(free, 1)
                    g_taken(dve, 1, L2, (layer, "conv", 4 + p))
                    for k in (2 * p, 2 * p + 1):
                        tap = [V_CONV + (3 * j + 2 - lag) * KT + k for lag in range(3)]
                        causal_conv(cv_c[:, k, :], cv_o[:, k, :], [v2[:, c:c + 1] for c in tap], None)
                for p in range(4):
                    bank, free = g_full_at(1, L2, (layer, "conv", 8 + p))
                    pair = slice(2 * p, 2 * p + 2)
                    dve.tensor_tensor(mix_y[:, pair, :], two(bank), cv_o[:, pair, :], ALU.mult).then_inc(free, 1)
                    conv_low_w(layer, 10 + p)
                    dve.wait_ge(y_high, 4 * j + p + 1)
                    dve.tensor_tensor(y_r[:, 1, pair, :], mix_y[:, pair, :], y_r[:, 0, pair, :], ALU.subtract)\
                        .then_inc(y_low, 1)

            def lru_mixer():
                dve.wait_ge(lam_exp, 1)
                lam = v2[:, V_LAM:V_LAM + LT]
                then(softplus_neg(L2, lam, *(lamb[:, n, :] for n in range(3, 8))))
                then(dve.tensor_scalar(lam8[:, 0:LT], lamb[:, 7, :], -8.0, None, ALU.mult))
                dve.tensor_scalar(lam8[:, LT:2 * LT], lamb[:, 7, :], 8.0, None, ALU.mult).then_inc(lam_ready, 1)
                for p in range(5):
                    g_taken(dve, 1, L2, (1, "rec", p))
                    for k in (2 * p, 2 * p + 1):
                        tap = [V_LCONV + (3 - lag) * LT + k for lag in range(4)]
                        causal_conv(r_raw[:, k, :], r_rec[:, k, :], [v2[:, c:c + 1] for c in tap],
                                    v2[:, V_LCB + k:V_LCB + k + 1], mix_ready)
                g_taken(dve, 1, L2, (1, "ri", LT - 2))
                g_taken(dve, 1, L2, (1, "ri", LT - 1))
                dve.wait_ge(mix_ready, LT)
                step(dve.tensor_tensor(r_i, r_i, r_rec, ALU.mult))
                settle(L2)
                for n in range(2):
                    s = slice(5 * n, 5 * n + 5)
                    dve.wait_ge(decay_exp, 5 * (n + 1))
                    then(dve.tensor_tensor(r_raw[:, s, :], r_a[:, s, :], r_a[:, s, :], ALU.mult))
                    dve.scalar_tensor_tensor(out=r_t[:, s, :], in0=r_raw[:, s, :], scalar=1.0, in1=r_t[:, s, :],
                                             op0=ALU.add, op1=ALU.mult).then_inc(var_ready, 1)
                for n in range(2):
                    s = slice(5 * n, 5 * n + 5)
                    dve.wait_ge(var_root, n + 1)
                    dve.wait_ge(var_ready, 2)
                    then(dve.tensor_tensor(r_i[:, s, :], r_i[:, s, :], r_t[:, s, :], ALU.mult))
                    for k in range(5 * n, 5 * n + 5):
                        step(dve.tensor_tensor_scan(out=r_raw[:, k, :], data0=r_a[:, k, :], data1=r_i[:, k, :],
                                                    initial=0.0, op0=ALU.mult, op1=ALU.add))
                settle(L2)
                for p in range(5):
                    g_taken(dve, 1, L2, (1, "gelu", p))
                    for k in (2 * p, 2 * p + 1):
                        dve.tensor_tensor(r_g[:, k, :], r_g[:, k, :], r_raw[:, k, :], ALU.mult).then_inc(mix_ready, 1)

            def rotary_angles():
                r = slice(0, ROPE)
                dve.wait_ge(pos_loaded, 16)
                then(dve.tensor_copy(rope_a[r, :], posi[:, :]))
                then(dve.tensor_scalar(rope_a[r, :], rope_a[r, :], cst[r, C_FREQ:C_FREQ + 1], None, ALU.mult))
                for n, (dst, turn) in enumerate(((cosT, 0.25), (sinT, 0.0))):
                    then(dve.tensor_scalar(rope_b[r, :], rope_a[r, :], 1 / TWO_PI, turn, ALU.mult, ALU.add))
                    then(dve.tensor_scalar(rope_b[r, :], rope_b[r, :], ROUND, None, ALU.add))
                    then(dve.tensor_scalar(rope_b[r, :], rope_b[r, :], -ROUND, None, ALU.add))
                    src = rope_a
                    for c in TWO_PI_PARTS:
                        then(dve.scalar_tensor_tensor(out=dst[r, :], in0=rope_b[r, :], scalar=-c, in1=src[r, :],
                                                      op0=ALU.mult, op1=ALU.add))
                        src = dst
                    then(dve.tensor_scalar(dst[r, :], dst[r, :], turn * TWO_PI, PI_BELOW, ALU.add, ALU.min))
                    dve.tensor_scalar(dst[r, :], dst[r, :], -PI_BELOW, None, ALU.max).then_inc(angle_ready, 1)

            def rope(name, t, count):
                r = slice(0, ROPE)
                bank, free = m_full_at(1, L2, name)
                if count:
                    dve.wait_ge(rope_ready, count)
                dve.tensor_tensor(rope_b[r, :], bank[r, 0:S], sinT[r, :], ALU.mult).then_inc(free, 1)
                step(dve.tensor_tensor(rope_c[r, :], t, cosT[r, :], ALU.mult))
                m_taken(dve, 1, L2, name)
                settle(L2)
                dve.tensor_tensor(t, rope_b[r, :], rope_c[r, :], ALU.add).then_inc(rope_ready, 1)

            def mla_mixer():
                scale = (NOPE + ROPE) ** -0.5
                then(dve.tensor_scalar(qgain[:, 0:1], v2[:, V_QNN:V_QNN + 1], scale, None, ALU.mult))
                then(dve.tensor_scalar(qgain[:, 1:2], v2[:, V_QRN:V_QRN + 1], scale, None, ALU.mult))
                rotary_angles()
                for i, (name, tiles_, rows, col) in enumerate((("cq", (0, 1, 2), P, V_QN), ("ckv", (3, 4), P, V_KVN),
                                                              ("kr", (5,), ROPE, V_KRN))):
                    m_taken(dve, 1, L2, (2, name))
                    then(dve.reciprocal(lroot[0:rows, i, :], lroot[0:rows, i, :]))
                    for n, k in enumerate(tiles_):
                        ins = dve.scalar_tensor_tensor(out=c_lat[0:rows, k, :], in0=c_lat[0:rows, k, :],
                                                       scalar=v2[0:rows, col + n:col + n + 1],
                                                       in1=lroot[0:rows, i, :], op0=ALU.mult, op1=ALU.mult)
                        if k == tiles_[-1]:
                            ins.then_inc(lat_ready, 1)
                        else:
                            step(ins)
                dve.wait_ge(sincos_ready, 2)
                dve.wait_ge(lat_ready, 3)
                rope((2, "krot"), c_lat[0:ROPE, 5, :], 0)
                for hd in range(HEADS + 1):
                    if hd < HEADS:
                        m_taken(dve, 1, L2, (2, "qn", hd))
                        s = hd % 2
                        step(dve.reciprocal(hsq[:, s, 0:S], hsq[:, s, 0:S]))
                        step(dve.reciprocal(hsq[0:ROPE, s, S:2 * S], hsq[0:ROPE, s, S:2 * S]))
                        settle(L2)
                        step(dve.scalar_tensor_tensor(out=qn[:, hd, :], in0=qn[:, hd, :], scalar=qgain[:, 0:1],
                                                      in1=hsq[:, s, 0:S], op0=ALU.mult, op1=ALU.mult))
                        dve.scalar_tensor_tensor(out=qr[0:ROPE, hd, :], in0=qr[0:ROPE, hd, :],
                                                 scalar=qgain[0:ROPE, 1:2], in1=hsq[0:ROPE, s, S:2 * S],
                                                 op0=ALU.mult, op1=ALU.mult).then_inc(head_ready, 1)
                    if hd >= 1:
                        rope((2, "qrot", hd - 1), qr[0:ROPE, hd - 1, :], hd)
                for hd in range(HEADS):
                    m_taken(dve, 1, L2, (2, "kn", hd))
                    s = hd % 2
                    then(dve.reciprocal(hsq[:, s, 0:S], hsq[:, s, 0:S]))
                    dve.scalar_tensor_tensor(out=kn[:, hd, :], in0=kn[:, hd, :], scalar=v2[:, V_KNN:V_KNN + 1],
                                             in1=hsq[:, s, 0:S], op0=ALU.mult, op1=ALU.mult).then_inc(head_ready, 1)
                for i in range(HEADS):
                    n = 2 * HEADS * LAYERS1 + i
                    soft_max(1, L2, (2, "s", i), n, i % 2, m_logit, causal[:, P:S], causal, i >= 2)
                    soft_norm(L2, n, i % 2, m_prob)

            magnitude(v2[:, V_LAM:V_LAM + LT], lamb[:, 2, :], lam_abs)
            for layer in range(LAYERS2):
                stage = 3 * LAYERS1 + 2 * layer
                mix_gain = v2[:, V_MIX + KT * layer:V_MIX + KT * (layer + 1)]
                ffn_gain = v2[:, V_FFN + KT * layer:V_FFN + KT * (layer + 1)]
                outs = [(layer, "out", p) for p in range(4)]
                if layer % 3 == 0:
                    if layer == 0:
                        conv_low_w(0, 0)
                    norm(1, L2, (layer, "norm", 0), mix_gain, h_scaled, (norms_split(layer, 0), None))
                    conv_low_w(layer, 1)
                    conv_mixer(layer)

                    def before_out(p):
                        if p < 2:
                            conv_low_w(layer, 14 + p)
                        elif p == 2:
                            low_w(1, L2, (layer, "gate", 0), 0)

                    residual(1, L2, outs, None, stage + 1, before=before_out)
                else:
                    norm(1, L2, (layer, "norm", 0), mix_gain, h_ready)
                    (None, lru_mixer, mla_mixer)[layer]()
                    residual(1, L2, outs, None, stage + 1, after=low_first(1, L2, (layer, "gate", 0)))
                norm(1, L2, (layer, "norm", 1), ffn_gain, h_scaled, (norms_split(layer, 1), None))
                if layer % 3 == 0:
                    low_w(1, L2, (layer, "gate", 0), 1)
                ffn(1, L2, (layer, "gate", 0), None, None, stage + 2, layer == LAYERS2 - 1,
                    layer + 1 if layer % 3 == 2 else None)


_STREAMED = ["w_ada", "ffn_w_gate", "ffn_w_up", "ffn_w_down", "w_in", "rel_bias", "w_branch", "w_out",
             "positions_2", "conv_w_in_2", "conv_w_out_2", "lru_w_in_2", "lru_gate_a_w_2", "lru_gate_x_w_2",
             "lru_w_out_2", "mla_w_down_2", "mla_w_uq_2", "mla_w_ukv_2", "mla_w_o_2", "ffn_w_gu_2",
             "ffn_w_down_2"]


def constants():
    c = np.zeros((P, C_ALL), np.float32)
    p = np.arange(P)
    c[:, C_IDENT:C_IDENT + P] = np.eye(P)
    c[:, C_HALVES:C_HALVES + P] = p[:, None] // DH == p[None, :] // DH
    c[:, C_ONES:C_ONES + S] = 1
    c[:, C_CAUSAL:C_CAUSAL + S] = np.where(np.arange(S)[None, :] - P > p[:, None], NEG, 0)
    for g, width in enumerate(WINDOWS):
        c[:, C_INV + S * g:C_INV + S * (g + 1)] = 1 / np.minimum(np.arange(S) + 1, width)
    for hd in range(HEADS):
        c[hd, C_SEL + P * hd:C_SEL + P * (hd + 1)] = 1
    half = ROPE // 2
    for n in range(half):
        c[n + half, C_ROT + n] = -1
        c[n, C_ROT + n + half] = 1
    c[:, C_FREQ] = 10000.0 ** (-2.0 * (p % half) / ROPE)
    c[:, C_EPS] = EPS
    return c


def columns(a):
    return a.reshape(-1, P).T


def padded(a):
    return np.pad(a.reshape(-1, 1), ((0, P - a.size), (0, 0)))


def kernel(**inputs):
    import concourse.bacc as bacc
    from concourse.bass_utils import run_bass_kernel_spmd

    a = {name: np.asarray(value) for name, value in inputs.items()}
    arrays = {name: np.ascontiguousarray(a[name]) for name in _STREAMED}
    arrays["x"] = np.ascontiguousarray(a["x"][0].reshape(S, KT, P).transpose(2, 1, 0))
    arrays["c"] = np.ascontiguousarray(columns(a["c"]))
    arrays["constants"] = constants()
    arrays["vectors_1"] = np.stack([np.concatenate([
        columns(a["b_ada"][l]), columns(a["norm_gain"][l]), np.tile(a["qk_gain"][l], (1, 2)).T,
        padded(a["forget_bias"][l]), columns(a["pool_scale"][l]),
        a["w_in"][l][:, 7 * MIX_COLS:G_COL].reshape(KT, P, HEADS).transpose(1, 0, 2).reshape(P, KT * HEADS),
        a["w_pool"][l].transpose(1, 0, 2).reshape(P, 4 * P)], axis=1) for l in range(LAYERS1)])
    arrays["vectors_2"] = np.concatenate([
        columns(a["mix_norm_2"]), columns(a["ffn_norm_2"]), columns(a["conv_w_2"]), columns(a["lru_conv_w_2"]),
        columns(a["lru_conv_b_2"]), columns(a["lru_gate_a_b_2"]), columns(a["lru_gate_x_b_2"]),
        columns(a["lru_lambda_2"]), columns(a["mla_q_norm_2"]), columns(a["mla_kv_norm_2"]),
        columns(a["mla_qn_norm_2"]), padded(a["mla_qr_norm_2"]), columns(a["mla_kn_norm_2"]),
        padded(a["mla_kr_norm_2"])], axis=1)

    nc = bacc.Bacc("TRN2", target_bir_lowering=False, num_devices=1)
    w = {}
    for name, array in arrays.items():
        w[name] = nc.dram_tensor("in_" + name, array.shape, mybir.dt.from_np(array.dtype), kind="ExternalInput").ap()
    out = nc.dram_tensor("out", (P, KT, S), F32, kind="ExternalOutput").ap()
    build_program(nc, w, out)
    r = run_bass_kernel_spmd(nc, [{"in_" + name: array for name, array in arrays.items()}], core_ids=[0])
    return r.results[0]["out"].transpose(2, 1, 0).reshape(1, S, D)
```
